# Optimizing a Trainium2 kernel written in Bass

```python
import math
import jax
import jax.numpy as jnp
from jax import lax
import numpy as np
import jax, jax.numpy as jnp

D_MODEL = 1024
BATCH = 1
SEQ = 256
DEPTH = 1

HEAD_DIM = 64
SCALE = HEAD_DIM ** -0.5
NEG_INF = -1e30
EPS = 1e-6
A_GROUPS = ((128, 1), (512, 4), (2048, 16))
A_HEADS_PER_GROUP = 4
A_HEADS = A_HEADS_PER_GROUP * len(A_GROUPS)
A_WIDTH = A_HEADS * HEAD_DIM
A_OUT = A_HEADS_PER_GROUP * HEAD_DIM
A_BLOCK = max(w // d for w, d in A_GROUPS)
LRU_WIDTH = D_MODEL // 2
LRU_BLOCKS = 8
LRU_BLOCK_DIM = LRU_WIDTH // LRU_BLOCKS
CONV_WIDTH = 4
LRU_C = 8.0
C_HEADS = 8
C_WIDTH = C_HEADS * HEAD_DIM
MOBA_BLOCK = 256
MOBA_TOPK = 3
MOBA_Q_CHUNK = 32
REL_BUCKETS = 32
REL_MAX_DIST = 2048
REL_HEADS = A_HEADS + C_HEADS
FFN_HIDDEN = -(-8 * D_MODEL // (3 * 256)) * 256
IN_SIZES = (A_WIDTH, A_WIDTH, A_WIDTH, LRU_WIDTH, LRU_WIDTH, C_WIDTH, C_WIDTH, C_WIDTH, 3 * D_MODEL)
IN_COLS = sum(IN_SIZES)


def rms_norm(x, g):
    xf = x.astype(jnp.float32)
    y = xf * lax.rsqrt(jnp.mean(xf * xf, axis=-1, keepdims=True) + EPS)
    return (y * g.astype(jnp.float32)).astype(x.dtype)

def rel_bucket(dist):
    max_exact = REL_BUCKETS // 2
    d = jnp.maximum(dist, 0)
    df = jnp.maximum(d, 1).astype(jnp.float32)
    large = max_exact + (jnp.log(df / max_exact) / math.log(REL_MAX_DIST / max_exact)
                         * (REL_BUCKETS - max_exact)).astype(jnp.int32)
    large = jnp.minimum(large, REL_BUCKETS - 1)
    return jnp.where(d < max_exact, d, large)

def dilated_window_attention(q, k, v, dilation, n_back, bias_tab):
    B, S, H, E = q.shape
    L = S // dilation
    nb = -(-L // A_BLOCK)
    Lp = nb * A_BLOCK

    def to_sub(t):
        t = t.reshape(B, L, dilation, H, E).transpose(0, 2, 3, 1, 4)
        t = jnp.pad(t, ((0, 0), (0, 0), (0, 0), (0, Lp - L), (0, 0)))
        return t.reshape(B, dilation, H, nb, A_BLOCK, E)

    qb, kb, vb = to_sub(q), to_sub(k), to_sub(v)

    def with_prev(t):
        prev = jnp.pad(t, ((0, 0), (0, 0), (0, 0), (1, 0), (0, 0), (0, 0)))[:, :, :, :nb]
        return jnp.concatenate([prev, t], axis=4)

    kk, vv = with_prev(kb), with_prev(vb)
    qi = jnp.arange(A_BLOCK)[:, None] + A_BLOCK
    kj = jnp.arange(2 * A_BLOCK)[None, :]
    delta = qi - kj
    band = (delta >= 0) & (delta <= n_back)
    has_prev = (jnp.arange(nb)[:, None, None] > 0) | (kj >= A_BLOCK)[None]
    valid = band[None] & has_prev
    bias = bias_tab.astype(jnp.float32)[rel_bucket(delta * dilation)]
    bias = jnp.transpose(bias, (2, 0, 1))
    logits = jnp.einsum('bdhnqe,bdhnke->bdhnqk', qb, kk).astype(jnp.float32) * SCALE
    logits = logits + bias[None, None, :, None]
    logits = jnp.where(valid[None, None, None], logits, NEG_INF)
    m = jnp.max(logits, axis=-1, keepdims=True)
    p = jnp.exp(logits - m)
    den = jnp.sum(p, axis=-1, keepdims=True)
    o = jnp.einsum('bdhnqk,bdhnke->bdhnqe', p, vv.astype(jnp.float32)) / den
    lse = (m + jnp.log(den))[..., 0]
    o = o.reshape(B, dilation, H, Lp, E)[:, :, :, :L].transpose(0, 3, 1, 2, 4).reshape(B, S, H, E)
    lse = lse.reshape(B, dilation, H, Lp)[:, :, :, :L].transpose(0, 3, 1, 2).reshape(B, S, H)
    return o, lse

def rg_lru_branch(xb, gb, conv_w, conv_b, w_a, b_a, w_x, b_x, lam):
    B, S, W = xb.shape
    xp = jnp.pad(xb, ((0, 0), (CONV_WIDTH - 1, 0), (0, 0)))
    xc = conv_b
    for i in range(CONV_WIDTH):
        xc = xc + xp[:, i:i + S] * conv_w[i]
    xr = xc.reshape(B, S, LRU_BLOCKS, LRU_BLOCK_DIM)
    r = jax.nn.sigmoid((jnp.einsum('bsnd,nde->bsne', xr, w_a).reshape(B, S, W) + b_a).astype(jnp.float32))
    ig = jax.nn.sigmoid((jnp.einsum('bsnd,nde->bsne', xr, w_x).reshape(B, S, W) + b_x).astype(jnp.float32))
    log_a = -LRU_C * r * jax.nn.softplus(-lam.astype(jnp.float32))
    a = jnp.exp(log_a)
    bterm = jnp.sqrt(-jnp.expm1(2.0 * log_a)) * (ig * xc.astype(jnp.float32))

    def combine(left, right):
        a1, b1 = left
        a2, b2 = right
        return a1 * a2, a2 * b1 + b2

    _, h = lax.associative_scan(combine, (a, bterm), axis=1)
    return (h * jax.nn.gelu(gb.astype(jnp.float32))).astype(xb.dtype)

def moba_attention(q, k, v, bias_tab):
    B, S, H, E = q.shape
    f32 = jnp.float32
    nblk = -(-S // MOBA_BLOCK)
    Sp = nblk * MOBA_BLOCK
    pad = ((0, 0), (0, 0), (0, Sp - S), (0, 0))
    qh = q.transpose(0, 2, 1, 3)
    qb = jnp.pad(qh, pad).reshape(B, H, nblk, MOBA_BLOCK, E)
    kb = jnp.pad(k.transpose(0, 2, 1, 3), pad).reshape(B, H, nblk, MOBA_BLOCK, E)
    vb = jnp.pad(v.transpose(0, 2, 1, 3), pad).reshape(B, H, nblk, MOBA_BLOCK, E)
    tab = bias_tab.astype(f32)
    off = jnp.arange(MOBA_BLOCK)
    delta = off[:, None] - off[None, :]
    bias_own = jnp.transpose(tab[rel_bucket(delta)], (2, 0, 1))
    lg = jnp.einsum('bhnqe,bhnke->bhnqk', qb, kb).astype(f32) * SCALE + bias_own[None, :, None]
    lg = jnp.where(delta >= 0, lg, NEG_INF)
    m_own = jnp.max(lg, axis=-1)
    p = jnp.exp(lg - m_own[..., None])
    den_own = jnp.sum(p, axis=-1).reshape(B, H, Sp)[:, :, :S]
    num_own = jnp.einsum('bhnqk,bhnke->bhnqe', p, vb.astype(f32)).reshape(B, H, Sp, E)[:, :, :S]
    m_own = m_own.reshape(B, H, Sp)[:, :, :S]
    n_sel = min(MOBA_TOPK, nblk - 1)
    if n_sel == 0:
        out = num_own / den_own[..., None]
    else:
        kmean = jnp.mean(kb.astype(f32), axis=3)
        qpos = jnp.arange(S)
        qblk = qpos // MOBA_BLOCK
        gate = jnp.einsum('bhse,bhne->bhsn', qh.astype(f32), kmean)
        gate = jnp.where(jnp.arange(nblk)[None, :] < qblk[:, None], gate, NEG_INF)
        _, idx = lax.top_k(gate, n_sel)
        base = (jnp.arange(B)[:, None] * H + jnp.arange(H)[None, :]) * nblk
        fidx = idx + base[:, :, None, None]
        kflat = kb.reshape(B * H * nblk, MOBA_BLOCK, E)
        vflat = vb.reshape(B * H * nblk, MOBA_BLOCK, E)
        head = jnp.arange(H)[None, :, None, None, None]
        tab_t = tab.T
        nq = S // MOBA_Q_CHUNK

        def chunks(t):
            return jnp.moveaxis(t.reshape(B, H, nq, MOBA_Q_CHUNK, *t.shape[3:]), 2, 0)

        def step(args):
            qc, fi, bi, qp, m_o, d_o, n_o = args
            ks = jnp.take(kflat, fi, axis=0)
            vs = jnp.take(vflat, fi, axis=0)
            lgs = jnp.einsum('bhqe,bhqnke->bhqnk', qc, ks).astype(f32) * SCALE
            kpos = bi[..., None] * MOBA_BLOCK + jnp.arange(MOBA_BLOCK)
            lgs = lgs + tab_t[head, rel_bucket(qp[:, None, None] - kpos)]
            ok = bi < (qp // MOBA_BLOCK)[:, None]
            lgs = jnp.where(ok[..., None], lgs, NEG_INF)
            mm = jnp.maximum(jnp.max(lgs, axis=(-2, -1)), m_o)
            ps = jnp.exp(lgs - mm[..., None, None])
            c_o = jnp.exp(m_o - mm)
            den = d_o * c_o + jnp.sum(ps, axis=(-2, -1))
            num = n_o * c_o[..., None] + jnp.einsum('bhqnk,bhqnke->bhqe', ps, vs.astype(f32))
            return num / den[..., None]

        out = lax.map(step, (chunks(qh), chunks(fidx), chunks(idx), qpos.reshape(nq, MOBA_Q_CHUNK),
                             chunks(m_own), chunks(den_own), chunks(num_own)))
        out = jnp.moveaxis(out, 0, 2).reshape(B, H, S, E)
    return out.transpose(0, 2, 1, 3)

def hybrid_layer(x, rel_bias, g_mix, w_in, conv_w, conv_b, lru_wa, lru_ba, lru_wx, lru_bx, lru_lam,
                 p_a, p_b, p_c, w_out, g_ffn, w_gu, w_down):
    B, S, D = x.shape
    h = rms_norm(x, g_mix)
    z = h @ w_in
    offs = np.cumsum(IN_SIZES)[:-1].tolist()
    qa, ka, va, xb, gb, qc, kc, vc, gates = jnp.split(z, offs, axis=-1)
    qa = qa.reshape(B, S, A_HEADS, HEAD_DIM)
    ka = ka.reshape(B, S, A_HEADS, HEAD_DIM)
    va = va.reshape(B, S, A_HEADS, HEAD_DIM)
    outs, lses = [], []
    for g, (window, dilation) in enumerate(A_GROUPS):
        sl = slice(g * A_HEADS_PER_GROUP, (g + 1) * A_HEADS_PER_GROUP)
        o, lse = dilated_window_attention(qa[:, :, sl], ka[:, :, sl], va[:, :, sl],
                                          dilation, window // dilation, rel_bias[:, sl])
        outs.append(o)
        lses.append(lse)
    wts = jax.nn.softmax(jnp.stack(lses, axis=0), axis=0)
    o_a = jnp.sum(wts[..., None] * jnp.stack(outs, axis=0), axis=0).reshape(B, S, A_OUT).astype(x.dtype)
    o_b = rg_lru_branch(xb, gb, conv_w, conv_b, lru_wa, lru_ba, lru_wx, lru_bx, lru_lam)
    o_c = moba_attention(qc.reshape(B, S, C_HEADS, HEAD_DIM), kc.reshape(B, S, C_HEADS, HEAD_DIM),
                         vc.reshape(B, S, C_HEADS, HEAD_DIM), rel_bias[:, A_HEADS:])
    o_c = o_c.reshape(B, S, C_WIDTH).astype(x.dtype)
    gt = jax.nn.sigmoid(gates.astype(jnp.float32)).astype(x.dtype).reshape(B, S, 3, D)
    merged = gt[:, :, 0] * (o_a @ p_a) + gt[:, :, 1] * (o_b @ p_b) + gt[:, :, 2] * (o_c @ p_c)
    x = x + merged @ w_out
    u = rms_norm(x, g_ffn) @ w_gu
    gate, up = jnp.split(u, 2, axis=-1)
    return x + (jax.nn.silu(gate) * up) @ w_down

def first_inputs(seed: int = 0) -> dict:
    key = jax.random.key(seed)
    ks = jax.random.split(key, 24)
    f32 = jnp.float32

    def nrm(k, shape, scale):
        return jax.random.normal(k, shape, f32) * scale

    u = jax.random.uniform(ks[11], (DEPTH, LRU_WIDTH), f32, 0.9, 0.999)
    a = u ** (1.0 / LRU_C)
    return {
        "x": nrm(ks[0], (BATCH, SEQ, D_MODEL), 1.0),
        "rel_bias": nrm(ks[1], (REL_BUCKETS, REL_HEADS), 0.5),
        "g_mix": 1.0 + nrm(ks[2], (DEPTH, D_MODEL), 0.05),
        "w_in": nrm(ks[3], (DEPTH, D_MODEL, IN_COLS), D_MODEL ** -0.5),
        "conv_w": nrm(ks[4], (DEPTH, CONV_WIDTH, LRU_WIDTH), CONV_WIDTH ** -0.5),
        "conv_b": nrm(ks[5], (DEPTH, LRU_WIDTH), 0.02),
        "lru_wa": nrm(ks[6], (DEPTH, LRU_BLOCKS, LRU_BLOCK_DIM, LRU_BLOCK_DIM), LRU_BLOCK_DIM ** -0.5),
        "lru_ba": nrm(ks[7], (DEPTH, LRU_WIDTH), 0.02),
        "lru_wx": nrm(ks[8], (DEPTH, LRU_BLOCKS, LRU_BLOCK_DIM, LRU_BLOCK_DIM), LRU_BLOCK_DIM ** -0.5),
        "lru_bx": nrm(ks[9], (DEPTH, LRU_WIDTH), 0.02),
        "lru_lam": jnp.log(a) - jnp.log1p(-a),
        "p_a": nrm(ks[12], (DEPTH, A_OUT, D_MODEL), A_OUT ** -0.5),
        "p_b": nrm(ks[13], (DEPTH, LRU_WIDTH, D_MODEL), LRU_WIDTH ** -0.5),
        "p_c": nrm(ks[14], (DEPTH, C_WIDTH, D_MODEL), C_WIDTH ** -0.5),
        "w_out": nrm(ks[15], (DEPTH, D_MODEL, D_MODEL), D_MODEL ** -0.5),
        "g_ffn": 1.0 + nrm(ks[16], (DEPTH, D_MODEL), 0.05),
        "w_gu": nrm(ks[17], (DEPTH, D_MODEL, 2 * FFN_HIDDEN), D_MODEL ** -0.5),
        "w_down": nrm(ks[18], (DEPTH, FFN_HIDDEN, D_MODEL), FFN_HIDDEN ** -0.5),
        "g_final": 1.0 + nrm(ks[19], (D_MODEL,), 0.05),
    }

def first_block(x, rel_bias, g_mix, w_in, conv_w, conv_b, lru_wa, lru_ba, lru_wx, lru_bx, lru_lam,
              p_a, p_b, p_c, w_out, g_ffn, w_gu, w_down, g_final):
    for l in range(DEPTH):
        x = hybrid_layer(x, rel_bias, g_mix[l], w_in[l], conv_w[l], conv_b[l], lru_wa[l], lru_ba[l],
                         lru_wx[l], lru_bx[l], lru_lam[l], p_a[l], p_b[l], p_c[l], w_out[l],
                         g_ffn[l], w_gu[l], w_down[l])
    return rms_norm(x, g_final)


DEPTH_2 = 2

ROPE_THETA = 10000.0
Q_BLOCK = 128
A_HEADS_2 = 8
A_KV_HEADS = 2
A_WINDOW = 128
B_HEADS = 4
IDX_HEADS = 4
IDX_DIM = 64
IDX_TOPK_MAX = 256
IDX_W_SCALE = (IDX_HEADS * IDX_DIM) ** -0.5
C_HEADS_2 = 4
C_NOPE = 64
C_ROPE = 32
C_V = 64
C_Q_RANK = 256
C_KV_RANK = 128
A_Q = A_HEADS_2 * HEAD_DIM
A_KV = A_KV_HEADS * HEAD_DIM
B_Q = B_HEADS * HEAD_DIM
B_KV = HEAD_DIM
IDX_Q = IDX_HEADS * IDX_DIM
IN_SPLITS = (A_Q, A_KV, A_KV, B_Q, B_KV, B_KV, IDX_Q, IDX_DIM, IDX_HEADS, C_Q_RANK, C_KV_RANK, C_ROPE)
IN_COLS_2 = A_Q + 2 * A_KV + B_Q + 2 * B_KV + IDX_Q + IDX_DIM + IDX_HEADS + C_Q_RANK + C_KV_RANK + C_ROPE
MIX_WIDTH = A_HEADS_2 * HEAD_DIM + B_HEADS * HEAD_DIM + C_HEADS_2 * C_V
N_EXPERTS = 16
N_GROUPS = 4
EXPERTS_PER_GROUP = N_EXPERTS // N_GROUPS
TOP_K = 2
D_EXPERT = 256
DEEPNORM_ALPHA = (2 * DEPTH_2) ** 0.25
DEEPNORM_BETA = (8 * DEPTH_2) ** -0.25
LN_EPS = 1e-5
RMS_EPS = 1e-6


def rope_tables(pos, dim):
    inv = 1.0 / (ROPE_THETA ** (jnp.arange(0, dim, 2, dtype=jnp.float32) / dim))
    ang = pos.astype(jnp.float32)[:, None] * inv[None, :]
    return jnp.cos(ang), jnp.sin(ang)

def apply_rope(x, cos, sin):
    d2 = x.shape[-1] // 2
    shape = (1, cos.shape[0]) + (1,) * (x.ndim - 3) + (d2,)
    c = cos.reshape(shape)
    s = sin.reshape(shape)
    xf = x.astype(jnp.float32)
    x1, x2 = xf[..., :d2], xf[..., d2:]
    return jnp.concatenate([x1 * c - x2 * s, x2 * c + x1 * s], axis=-1).astype(x.dtype)

def layer_norm(x, g, b):
    xf = x.astype(jnp.float32)
    mu = jnp.mean(xf, axis=-1, keepdims=True)
    var = jnp.mean(jnp.square(xf - mu), axis=-1, keepdims=True)
    return ((xf - mu) * lax.rsqrt(var + LN_EPS) * g.astype(jnp.float32) + b.astype(jnp.float32)).astype(x.dtype)

def rms_norm_2(x, g):
    xf = x.astype(jnp.float32)
    return (xf * lax.rsqrt(jnp.mean(jnp.square(xf), axis=-1, keepdims=True) + RMS_EPS) * g.astype(jnp.float32)).astype(x.dtype)

def split_cols(h):
    offs = np.cumsum(IN_SPLITS)[:-1].tolist()
    return jnp.split(h, offs, axis=-1)

def to_blocks(t):
    b, s = t.shape[0], t.shape[1]
    return jnp.moveaxis(t.reshape((b, s // Q_BLOCK, Q_BLOCK) + t.shape[2:]), 1, 0)

def sliding_window_sink_attn(q, k, v, sinks):
    B, S, Hq, D = q.shape
    Hkv = k.shape[2]
    G = Hq // Hkv
    W = A_WINDOW
    nb = S // W
    qb = q.reshape(B, nb, W, Hkv, G, D)

    def band(t):
        tb = t.reshape(B, nb, W, Hkv, D)
        prev = jnp.pad(tb[:, :-1], ((0, 0), (1, 0), (0, 0), (0, 0), (0, 0)))
        return jnp.concatenate([prev, tb], axis=2)

    kb, vb = band(k), band(v)
    s = jnp.einsum('bnqhgd,bnkhd->bnhgqk', qb, kb).astype(jnp.float32) * (D ** -0.5)
    qi = jnp.arange(W)[:, None]
    kj = jnp.arange(2 * W)[None, :]
    diff = qi + W - kj
    in_window = (diff >= 0) & (diff < W)
    not_pad = (jnp.arange(nb)[:, None, None] > 0) | (kj[None] >= W)
    mask = (in_window[None] & not_pad)[None, :, None, None]
    s = jnp.where(mask, s, -jnp.inf)
    sink = jnp.broadcast_to(sinks.astype(jnp.float32).reshape(1, 1, Hkv, G, 1, 1), s.shape[:-1] + (1,))
    p = jax.nn.softmax(jnp.concatenate([s, sink], axis=-1), axis=-1)[..., :-1]
    o = jnp.einsum('bnhgqk,bnkhd->bnqhgd', p.astype(v.dtype), vb)
    return o.reshape(B, S, Hq * D)

def indexer_sparse_attn(q, k, v, q_idx, k_idx, w_idx):
    B, S, H, D = q.shape
    topk = min(IDX_TOPK_MAX, S // 4)
    nb = S // Q_BLOCK
    key_pos = jnp.arange(S)
    bidx = jnp.arange(B)[:, None]

    def block_fn(args):
        qb, qib, wb, t0 = args
        tpos = t0 + jnp.arange(Q_BLOCK)
        logits = jnp.einsum('bthd,bsd->bths', qib, k_idx).astype(jnp.float32)
        score = jnp.einsum('bth,bths->bts', wb.astype(jnp.float32), jax.nn.relu(logits))
        causal = key_pos[None, :] <= tpos[:, None]
        score = jnp.where(causal[None], score, -jnp.inf)
        _, idx = lax.top_k(score, topk)
        flat = idx.reshape(B, Q_BLOCK * topk)
        kg = k[bidx, flat].reshape(B, Q_BLOCK, topk, D)
        vg = v[bidx, flat].reshape(B, Q_BLOCK, topk, D)
        valid = idx <= tpos[None, :, None]
        s = jnp.einsum('bthd,btkd->bthk', qb, kg).astype(jnp.float32) * (D ** -0.5)
        s = jnp.where(valid[:, :, None, :], s, -jnp.inf)
        p = jax.nn.softmax(s, axis=-1)
        return jnp.einsum('bthk,btkd->bthd', p.astype(vg.dtype), vg)

    t0s = jnp.arange(nb, dtype=jnp.int32) * Q_BLOCK
    out = lax.map(block_fn, (to_blocks(q), to_blocks(q_idx), to_blocks(w_idx), t0s))
    return jnp.moveaxis(out, 0, 1).reshape(B, S, H * D)

def mla_attn(q_nope, q_rope, k_nope, k_rope, v):
    B, S, H, Dv = v.shape
    scale = (q_nope.shape[-1] + q_rope.shape[-1]) ** -0.5
    nb = S // Q_BLOCK
    key_pos = jnp.arange(S)

    def block_fn(args):
        qn, qr, t0 = args
        tpos = t0 + jnp.arange(Q_BLOCK)
        s = (jnp.einsum('bthd,bshd->bhts', qn, k_nope) + jnp.einsum('bthd,bsd->bhts', qr, k_rope)).astype(jnp.float32) * scale
        causal = key_pos[None, :] <= tpos[:, None]
        s = jnp.where(causal[None, None], s, -jnp.inf)
        p = jax.nn.softmax(s, axis=-1)
        return jnp.einsum('bhts,bshd->bthd', p.astype(v.dtype), v)

    t0s = jnp.arange(nb, dtype=jnp.int32) * Q_BLOCK
    out = lax.map(block_fn, (to_blocks(q_nope), to_blocks(q_rope), t0s))
    return jnp.moveaxis(out, 0, 1).reshape(B, S, H * Dv)

def moe_ffn(x, w_router, router_bias, w_gate, w_up, w_down):
    B, S, D = x.shape
    N = B * S
    xt = x.reshape(N, D)
    scores = jax.nn.sigmoid(jnp.dot(xt, w_router).astype(jnp.float32))
    biased = (scores + router_bias.astype(jnp.float32)).reshape(N, N_GROUPS, EXPERTS_PER_GROUP)
    group_score = jnp.sum(lax.top_k(biased, TOP_K)[0], axis=-1)
    g_sel = jnp.argmax(group_score, axis=-1)
    in_group = jnp.take_along_axis(biased, g_sel[:, None, None], axis=1)[:, 0]
    _, local = lax.top_k(in_group, TOP_K)
    expert_idx = g_sel[:, None] * EXPERTS_PER_GROUP + local
    w = jnp.take_along_axis(scores, expert_idx, axis=1)
    w = w / jnp.sum(w, axis=-1, keepdims=True)
    gates = jnp.sum(jax.nn.one_hot(expert_idx, N_EXPERTS, dtype=jnp.float32) * w[..., None], axis=1)
    h = jax.nn.silu(jnp.einsum('nd,edf->enf', xt, w_gate)) * jnp.einsum('nd,edf->enf', xt, w_up)
    h = h * gates.T.astype(h.dtype)[:, :, None]
    y = jnp.einsum('enf,efd->nd', h, w_down)
    return y.reshape(B, S, D)

def second_inputs(seed: int = 0) -> dict:
    key = jax.random.key(seed)
    ks = jax.random.split(key, 20)
    f32 = jnp.float32
    nrm = lambda k, shape, scale: jax.random.normal(k, shape, f32) * scale
    return {
        'x': nrm(ks[0], (BATCH, SEQ, D_MODEL), 1.0),
        'w_in': nrm(ks[1], (DEPTH_2, D_MODEL, IN_COLS_2), D_MODEL ** -0.5),
        'attn_sinks': nrm(ks[2], (DEPTH_2, A_HEADS_2), 0.5),
        'c_q_norm_g': 1.0 + nrm(ks[3], (DEPTH_2, C_Q_RANK), 0.02),
        'c_kv_norm_g': 1.0 + nrm(ks[4], (DEPTH_2, C_KV_RANK), 0.02),
        'w_uq': nrm(ks[5], (DEPTH_2, C_Q_RANK, C_HEADS_2 * (C_NOPE + C_ROPE)), C_Q_RANK ** -0.5),
        'w_ukv': nrm(ks[6], (DEPTH_2, C_KV_RANK, C_HEADS_2 * (C_NOPE + C_V)), C_KV_RANK ** -0.5),
        'w_out': nrm(ks[7], (DEPTH_2, MIX_WIDTH, D_MODEL), DEEPNORM_BETA * MIX_WIDTH ** -0.5),
        'ln1_g': 1.0 + nrm(ks[8], (DEPTH_2, D_MODEL), 0.02),
        'ln1_b': nrm(ks[9], (DEPTH_2, D_MODEL), 0.02),
        'w_router': nrm(ks[10], (D_MODEL, N_EXPERTS), D_MODEL ** -0.5),
        'router_bias': nrm(ks[11], (N_EXPERTS,), 0.01),
        'w_gate': nrm(ks[12], (DEPTH_2, N_EXPERTS, D_MODEL, D_EXPERT), D_MODEL ** -0.5),
        'w_up': nrm(ks[13], (DEPTH_2, N_EXPERTS, D_MODEL, D_EXPERT), D_MODEL ** -0.5),
        'w_down': nrm(ks[14], (DEPTH_2, N_EXPERTS, D_EXPERT, D_MODEL), DEEPNORM_BETA * D_EXPERT ** -0.5),
        'ln2_g': 1.0 + nrm(ks[15], (DEPTH_2, D_MODEL), 0.02),
        'ln2_b': nrm(ks[16], (DEPTH_2, D_MODEL), 0.02),
    }

def second_block(x, w_in, attn_sinks, c_q_norm_g, c_kv_norm_g, w_uq, w_ukv, w_out, ln1_g, ln1_b, w_router, router_bias, w_gate, w_up, w_down, ln2_g, ln2_b):
    B, S, _ = x.shape
    pos = jnp.arange(S)
    cos_h, sin_h = rope_tables(pos, HEAD_DIM)
    cos_r, sin_r = rope_tables(pos, C_ROPE)
    for l in range(DEPTH_2):
        h = jnp.einsum('bsd,dc->bsc', x, w_in[l])
        a_q, a_k, a_v, b_q, b_k, b_v, i_q, i_k, i_w, c_q, c_kv, c_kr = split_cols(h)
        o_a = sliding_window_sink_attn(
            apply_rope(a_q.reshape(B, S, A_HEADS_2, HEAD_DIM), cos_h, sin_h),
            apply_rope(a_k.reshape(B, S, A_KV_HEADS, HEAD_DIM), cos_h, sin_h),
            a_v.reshape(B, S, A_KV_HEADS, HEAD_DIM), attn_sinks[l])
        o_b = indexer_sparse_attn(
            apply_rope(b_q.reshape(B, S, B_HEADS, HEAD_DIM), cos_h, sin_h),
            apply_rope(b_k, cos_h, sin_h), b_v,
            apply_rope(i_q.reshape(B, S, IDX_HEADS, IDX_DIM), cos_h, sin_h),
            apply_rope(i_k, cos_h, sin_h), i_w * IDX_W_SCALE)
        q_c = jnp.einsum('bsr,rc->bsc', rms_norm_2(c_q, c_q_norm_g[l]), w_uq[l]).reshape(B, S, C_HEADS_2, C_NOPE + C_ROPE)
        kv_c = jnp.einsum('bsr,rc->bsc', rms_norm_2(c_kv, c_kv_norm_g[l]), w_ukv[l]).reshape(B, S, C_HEADS_2, C_NOPE + C_V)
        o_c = mla_attn(q_c[..., :C_NOPE], apply_rope(q_c[..., C_NOPE:], cos_r, sin_r),
                       kv_c[..., :C_NOPE], apply_rope(c_kr, cos_r, sin_r), kv_c[..., C_NOPE:])
        mix = jnp.concatenate([o_a, o_b, o_c], axis=-1)
        x = layer_norm(DEEPNORM_ALPHA * x + jnp.einsum('bsm,md->bsd', mix, w_out[l]), ln1_g[l], ln1_b[l])
        x = layer_norm(DEEPNORM_ALPHA * x + moe_ffn(x, w_router, router_bias, w_gate[l], w_up[l], w_down[l]), ln2_g[l], ln2_b[l])
    return x


def setup_inputs(seed=0):
    out = dict(first_inputs(seed))
    for name, value in second_inputs(seed + 1).items():
        if name != "x":
            out[name + "_2"] = value
    return out


def reference(
    x, rel_bias, g_mix, w_in, conv_w, conv_b, lru_wa, lru_ba, lru_wx, lru_bx, lru_lam, p_a, p_b,
    p_c, w_out, g_ffn, w_gu, w_down, g_final, w_in_2, attn_sinks_2, c_q_norm_g_2, c_kv_norm_g_2,
    w_uq_2, w_ukv_2, w_out_2, ln1_g_2, ln1_b_2, w_router_2, router_bias_2, w_gate_2, w_up_2,
    w_down_2, ln2_g_2, ln2_b_2,
):
    x = first_block(
        x, rel_bias, g_mix, w_in, conv_w, conv_b, lru_wa, lru_ba, lru_wx, lru_bx, lru_lam, p_a,
        p_b, p_c, w_out, g_ffn, w_gu, w_down, g_final,
    )
    return second_block(
        x, w_in_2, attn_sinks_2, c_q_norm_g_2, c_kv_norm_g_2, w_uq_2, w_ukv_2, w_out_2, ln1_g_2,
        ln1_b_2, w_router_2, router_bias_2, w_gate_2, w_up_2, w_down_2, ln2_g_2, ln2_b_2,
    )


_drawn_inputs = setup_inputs


def setup_inputs(seed=0):
    import zlib

    import numpy as np

    out = dict(_drawn_inputs(seed))
    spreads = {}
    factors = {'lru_ba': 8.0,
     'lru_bx': 6.514,
     'attn_sinks_2': 5.63,
     'c_q_norm_g_2': 4.216,
     'c_kv_norm_g_2': 8.0}
    for name, (base, spread) in spreads.items():
        noise = np.random.default_rng([zlib.crc32(name.encode()), seed]).standard_normal(out[name].shape)
        drawn = base * np.exp(spread * noise) if base else spread * noise
        out[name] = jnp.asarray(drawn.astype(out[name].dtype))
    for name, factor in factors.items():
        out[name] = (out[name] * factor).astype(out[name].dtype)
    return out
```

```python
import math
from contextlib import ExitStack

import numpy as np

import concourse.bass as bass
from concourse import mybir

F32 = mybir.dt.float32
F32R = mybir.dt.float32r
ALU = mybir.AluOpType
ACT = mybir.ActivationFunctionType
AX = mybir.AxisListType

P = 128
S = 256
TT = S // P
D = 1024
KD = D // P
NEG = -1e30
SEL = -3e38

HD = 64
A_HEADS, A_GROUPS, A_PER = 12, 3, 4
C_HEADS = 8
LRU = 512
LC = LRU // P
FFN = 2816
REL_BUCKETS, REL_MAX = 32, 2048
DILATIONS = (1, 4, 16)
N_BACK = 128
EPS_RMS = 1e-6
SCALE = HD ** -0.5

LAYERS = 2
IN2 = 1892
N_EXP, D_EXP = 16, 256
IDX_HEADS = 4
IDX_W_SCALE = (4 * 64) ** -0.5
IDX_TOPK = 64
C2_SCALE = 96 ** -0.5
ALPHA = (2 * LAYERS) ** 0.25
EPS_LN = 1e-5
C_QR, C_KVR = 256, 128
AQ, AK, AV, BQ, BK, BV, IQ, IK, IW, CQ, CKV, CKR = 0, 512, 640, 768, 1024, 1088, 1152, 1408, 1472, 1476, 1732, 1860

TW = 2048
COL_TILES = [0, 3, 6, 1, 4, 7, 2, 5, 8] + list(range(9, 31))
N_COL = len(COL_TILES)
G_LATE = 28
T_PA, T_PB, T_PC, T_WO = 31, 32, 34, 36
T_FFN = 40
FFN_E = FFN // 256
T_L = T_FFN + 3 * FFN_E
L_TILES = 63
L_COLS = [0, 1, 2, 4, 5, 6, 7, 3]
L_WIDTHS = [min(256, IN2 - tile * 256) for tile in L_COLS]
J_UQ, J_UKV, J_WO, J_RT, J_MOE = 8, 9, 10, 14, 15

U_L0, U_PER = 14, 12


def rel_bucket(dist):
    max_exact = REL_BUCKETS // 2
    d = np.maximum(dist, 0)
    df = np.maximum(d, 1).astype(np.float32)
    large = max_exact + (np.log(df / np.float32(max_exact)) / np.float32(math.log(REL_MAX / max_exact))
                         * np.float32(REL_BUCKETS - max_exact)).astype(np.int32)
    return np.where(d < max_exact, d, np.minimum(large, REL_BUCKETS - 1))


C_ID, C_MC, C_MA, C_CC, C_SS, C_CC16, C_SS16, C_TRI = 0, 128, 384, 640, 768, 896, 960, 1024
C_ALL = 1152
POOL_LINKS, DVE_LINKS, PE_LINKS = 19, 156, 11


def shape_constants():
    c = np.zeros((P, C_ALL), np.float32)
    c[:, C_ID:C_ID + P] = np.eye(P)
    delta = np.arange(P)[:, None] + P - np.arange(S)[None, :]
    c[:, C_MC:C_MC + S] = np.where(delta >= 0, 0, NEG)
    c[:, C_MA:C_MA + S] = np.where((delta >= 0) & (delta < 128), 0, NEG)
    pos = np.arange(S).astype(np.float32)
    for dim, cc, ss in ((64, C_CC, C_SS), (32, C_CC16, C_SS16)):
        inv = (1.0 / (10000.0 ** (np.arange(0, dim, 2, dtype=np.float32) / np.float32(dim)))).astype(np.float32)
        ang = pos[:, None] * inv[None, :]
        co, si = np.cos(ang), np.sin(ang)
        c[:, cc:cc + 2 * dim] = np.concatenate([co, co], 1).reshape(TT, P, dim).transpose(1, 0, 2).reshape(P, -1)
        c[:, ss:ss + 2 * dim] = np.concatenate([-si, si], 1).reshape(TT, P, dim).transpose(1, 0, 2).reshape(P, -1)
    c[:, C_TRI:C_TRI + 16] = (np.arange(4)[None, :] < np.arange(4)[:, None]).astype(np.float32).reshape(-1)
    dist = S - 1 - np.arange(2 * S)
    oh = np.zeros((REL_BUCKETS + 4, 2 * S), np.float32)
    oh[:REL_BUCKETS] = (rel_bucket(dist)[None] == np.arange(REL_BUCKETS)[:, None]) & (dist >= 0)[None]
    for g, d in enumerate(DILATIONS):
        oh[REL_BUCKETS + g] = np.where((dist >= 0) & (dist % d == 0) & (dist <= N_BACK * d), 0, NEG)
    oh[REL_BUCKETS + 3] = np.where(dist >= 0, 0, NEG)
    ind = np.zeros((4, A_HEADS + C_HEADS), np.float32)
    for h in range(A_HEADS):
        ind[h // A_PER, h] = 1
    ind[3, A_HEADS:] = 1
    return {"shape_consts": c, "shape_buckets": oh, "shape_groups": ind}


def spread(ap, at, n):
    dims = [list(x) for x in ap.ap]
    dims.insert(at, [0, n])
    return bass.AP(ap.tensor, ap.offset, dims)


def backward(ap):
    dims = [list(x) for x in ap.ap]
    step, n = dims[-1]
    return bass.AP(ap.tensor, ap.offset + step * (n - 1), dims[:-1] + [[-step, n]])


def rows_of(ap, n=P):
    return bass.AP(ap.tensor, ap.offset, [[0, n]] + [list(x) for x in ap.ap])


class Chain:

    def __init__(self, eng, sem, base=0, per=0, turn=0):
        self.eng, self.sem, self.base, self.per, self.turn, self.n = eng, sem, base, per, turn, 0

    def __call__(self, ins, apart=None):
        self.n += 1
        ins.then_inc(self.sem, 1)
        if apart:
            apart(self.eng, self.sem, self.turn * self.per + (self.base + self.n))
        else:
            self.wait()

    def wait(self):
        self.eng.wait_ge(self.sem, self.turn * self.per + (self.base + self.n))


def build(nc, I, out):
    with ExitStack() as ctx:
        def sb(name, shape, dt=F32):
            return ctx.enter_context(nc.sbuf_tensor(name, shape, dt))

        def sem(name):
            return ctx.enter_context(nc.semaphore(name))

        ps = ctx.enter_context(nc.psum_tensor("ps", [P, 8, 512], F32))

        def banks(a, b):
            return ps[:, a:b, :].rearrange("p a b -> p (a b)")

        raw = sb("raw", [P, 3, TW])
        whi = sb("whi", [P, 3, TW], F32R)
        wlo = sb("wlo", [P, 3, TW], F32R)
        act_hi = sb("act_hi", [P, KD, S], F32R)
        act_lo = sb("act_lo", [P, KD, S], F32R)
        mix_hi = sb("mix_hi", [P, 10, S], F32R)
        mix_lo = sb("mix_lo", [P, 10, S], F32R)
        hid_hi, hid_lo = mix_hi[:, 8:10, :], mix_lo[:, 8:10, :]
        x_tok = sb("x_tok", [P, TT, D])
        cst = sb("cst", [P, C_ALL])
        pbuf = sb("pbuf", [P, 2, 768])
        pt = sb("pt", [P, 768])
        small = sb("small", [P, 360])
        arena_w = 30 * 256 + 20 * 256 + 20 * 256 + 16
        arena = sb("arena", [P, arena_w])

        ident = cst[:, C_ID:C_ID + P]

        def carve(at, *shape):
            n = int(np.prod(shape))
            assert at + n <= arena_w
            v = arena[:, at:at + n]
            if len(shape) == 2:
                return v.rearrange("p (a b) -> p a b", a=shape[0])
            if len(shape) == 3:
                return v.rearrange("p (a b c) -> p a b c", a=shape[0], b=shape[1])
            return v

        R1, R2, R3 = 0, 30 * 256, 50 * 256
        qa = carve(R1, 6, S)
        ka = carve(R1 + 1536, 6, S)
        va = carve(R1 + 3072, TT, A_HEADS * HD)
        bias_a = carve(R1 + 4608, A_GROUPS, A_PER, S)
        gates = carve(R1, 24, S)
        gelu_t = carve(R1 + 6144, LC * S)
        bias_c = carve(R2, C_HEADS, S)
        qc = carve(R2 + 2048, 4, S)
        kc = carve(R2 + 3072, 4, S)
        vc = carve(R2 + 4096, TT, C_HEADS * HD)
        merged = carve(R2, KD, S)
        xn2 = carve(R2 + 2048, TT, D)
        g_ffn = carve(R2 + 4096, D)
        LP = S + 4
        xbp = carve(R3, LC, LP)
        lru_th = gelu_t
        gb = carve(R3 + 1040, LC, S)
        xc = carve(R3 + 2064, LC, S)
        rr = carve(R3 + 3088, LC, S)
        ig = carve(R3 + 4112, LC, S)
        xn1 = carve(R3 + 16, TT, D)
        g_mix = carve(R3 + 16 + 2048, D)
        g_fin = carve(R3 + 3088, D)
        lru_q = pbuf[:, :, :].rearrange("p a b -> p (a b)")[:, 0:LC * S]
        o_a = sb("o_a", [P, TT, A_PER * HD])
        o_c = carve(R3, TT, C_HEADS * HD)

        hw = 1920
        h = carve(0, TT, hw)
        gate_bc = carve(0, N_EXP, S)
        o0 = N_EXP * S
        iq_t = carve(o0, 2, S)
        ik_t = carve(o0 + 512, S)
        bq_t = carve(o0 + 768, 2, S)
        bk_t = carve(o0 + 1280, S)
        aq_t = carve(o0 + 1536, 4, S)
        ak_t = carve(o0 + 2560, 2, S)
        o1 = o0 + 3072
        cn = carve(o1, TT, C_QR + C_KVR)
        q_c = carve(o1 + 768, TT, 384)
        kv_c = carve(o1 + 1536, TT, 512)
        kcat = carve(o1 + 2560, TT, 4, 96)
        qc_t = carve(o1 + 3328, 4, S)
        twice = [carve(o1 + 3328, TT, P), carve(o1 + 10240, TT, P), carve(o1 + 3840, TT, P), carve(o1 + 4096, TT, P)]
        kc_t = carve(o1 + 4352, 4, S)
        ln_g = carve(o1 + 3328, D)
        ln_b = carve(o1 + 4352, D)
        mix_tok = carve(o1 + 5376, TT, D)
        o2 = o1 + 7424
        score = carve(o2, 384)
        pick = carve(o2 + 384, 384)
        mask_b = carve(o2 + 768, 384)
        rope_a = carve(o2 + 1152, 640)
        rope_b = carve(o2 + 1792, 640)
        c_g = carve(o2 + 2432, C_QR + C_KVR)
        e_silu = carve(o1, 512)
        e_t = carve(o1 + 512, 512)
        relu_t = [pbuf[:, :, :].rearrange("p a b -> p (a b)")[:, 0:1024], pbuf[:, :, :].rearrange("p a b -> p (a b)")[:, 1024:1536]]

        f_silu = carve(R1, 512)
        f_t = carve(R1 + 512, 512)

        sm_at = [0]

        def tiny(n):
            v = small[:, sm_at[0]:sm_at[0] + n]
            sm_at[0] += n
            assert sm_at[0] <= 360
            return v

        st = tiny(24).rearrange("p (a b) -> p a b", a=2)
        mv = tiny(4).rearrange("p (a b) -> p a b", a=2)
        var = tiny(2)
        rstd = tiny(2)
        mhalf = tiny(4)
        negm = tiny(16).rearrange("p (a b) -> p a b", a=4)
        den = tiny(16).rearrange("p (a b) -> p a b", a=4)
        esink = tiny(16).rearrange("p (a b) -> p a b", a=4)
        rden = tiny(16).rearrange("p (a b) -> p a b", a=4)
        sinks = tiny(8)
        nsink = tiny(8)
        best = tiny(8)
        wi = tiny(8).rearrange("p (a b) -> p a b", a=2)
        cst4 = tiny(24).rearrange("p (a b) -> p a b", a=4)
        cvar = tiny(4)
        crstd = tiny(4)
        rbias = tiny(16)
        rt = [tiny(32).rearrange("p (a b) -> p a b", a=2) for _ in range(3)]
        rg = [tiny(8).rearrange("p (a b) -> p a b", a=2) for _ in range(3)]
        rs = tiny(4)
        pair = sb("pair", [P, 160])
        prm = pbuf[:, :, :].rearrange("p a b -> p (a b)")[0:8, 512:1024]
        prm_t = sb("prm_t", [P, LC, 8])
        lam = sb("lam", [P, 8, LC])
        bd_a = cst[:, 128:640].rearrange("p (c e) -> p c e", c=LC)
        bd_x = cst[:, 640:1152].rearrange("p (c e) -> p c e", c=LC)
        buck = pbuf[:, :, :].rearrange("p a b -> p (a b)")[0:36, 0:512]
        tabx = sb("tabx", [36, 20])
        ext = pt[0:20, 0:512]
        gt_sb = pt[0:16, 0:S]

        bias_dram = nc.dram_tensor("bias_rows", (20, 2 * S), F32, kind="Internal")
        gate_dram = nc.dram_tensor("gate_rows", (N_EXP, S), F32, kind="Internal")

        raw_in = [sem(f"raw_in{i}") for i in range(3)]
        hi_made, lo_made, tile_used = sem("hi_made"), sem("lo_made"), sem("tile_used")
        ring_free = sem("ring_free")
        p_read = sem("p_read")
        lay_in, c2_in = sem("lay_in"), sem("c2_in")
        tok_ready = sem("tok_ready")
        tr_full, tr_hi, tr_lo = sem("tr_full"), sem("tr_hi"), sem("tr_lo")
        var_ready, rstd_ready = sem("var_ready"), sem("rstd_ready")
        x_in, c_in, init_in, prm_in, lru_in, gln_in = (sem("x_in"), sem("c_in"), sem("init_in"), sem("prm_in"),
                                                       sem("lru_in"), sem("gln_in"))
        g_in = sem("g_in")
        gmix_in = sem("gmix_in")
        bd_zero, pad_zero = sem("bd_zero"), sem("pad_zero")
        mhalf_set = sem("mhalf_set")
        ext_full, ext_sb, ext_out, bias_in = sem("ext_full"), sem("ext_sb"), sem("ext_out"), sem("bias_in")
        prm_full, prm_sb = sem("prm_full"), sem("prm_sb")
        sc_full, l_ready, p_ready, pt_full, pt_ready, pv_full, o_ready = (
            sem("sc_full"), sem("l_ready"), sem("p_ready"), sem("pt_full"), sem("pt_ready"), sem("pv_full"), sem("o_ready"))
        lam_abs, lam_exp = sem("lam_abs"), sem("lam_exp")
        xc_ready, lru_full, lru_gates, la_ready, a_ready, om_ready, sq_ready, hb_ready, hb_hi, hb_lo = (
            sem("xc_ready"), sem("lru_full"), sem("lru_gates"), sem("la_ready"), sem("a_ready"), sem("om_ready"),
            sem("sq_ready"), sem("hb_ready"), sem("hb_hi"), sem("hb_lo"))
        gelu_in, gelu_tanh, gelu_done, rden_b1 = sem("gelu_in"), sem("gelu_tanh"), sem("gelu_done"), sem("rden_b1")
        ot_full, ot_hi, ot_lo = sem("ot_full"), sem("ot_hi"), sem("ot_lo")
        m_ready, m_hi, m_lo = sem("m_ready"), sem("m_hi"), sem("m_lo")
        g_full, u_full, silu_done, t_ready, hid_h, hid_l = (
            sem("g_full"), sem("u_full"), sem("silu_done"), sem("t_ready"), sem("hid_h"), sem("hid_l"))
        rope_done = sem("rope_done")
        tb_full, tb_free, cn_hi, cn_lo = sem("tb_full"), sem("tb_free"), sem("cn_hi"), sem("cn_lo")
        idx_full, idx_relu, mask_ready = sem("idx_full"), sem("idx_relu"), sem("mask_ready")
        cn_var, cn_rstd, cn_ready = sem("cn_var"), sem("cn_rstd"), sem("cn_ready")
        ukv_full, ukv_sb, kcat_ready = sem("ukv_full"), sem("ukv_sb"), sem("kcat_ready")
        sink_l, sink_e = sem("sink_l"), sem("sink_e")
        rt_full, rt_exp, gts_ready, gt_full, gt_ready, gt_out, gate_in = (
            sem("rt_full"), sem("rt_exp"), sem("gts_ready"), sem("gt_full"), sem("gt_ready"), sem("gt_out"), sem("gate_in"))
        dve_seq, dve_seq_l, dve_seq_e, act_seq, act_seq_l, pool_seq, pool_seq_l = (
            sem("dve_seq"), sem("dve_seq_l"), sem("dve_seq_e"), sem("act_seq"), sem("act_seq_l"), sem("pool_seq"),
            sem("pool_seq_l"))
        g_sig = sem("g_sig")
        early_out = sem("early_out")
        pe_seq, pe_seq_l = sem("pe_seq"), sem("pe_seq_l")
        out_done = sem("out_done")

        block = ctx.enter_context(nc.Block())

        def apart(eng, semaphore, value):
            if isinstance(value, int):
                eng.wait_ge(semaphore, value)
                return
            with eng.register() as awaited:
                eng.reg_mov(awaited, value)
                eng.wait_ge(c_in, 16)
                eng.wait_ge(semaphore, awaited)

        def unit_first(u):
            if u < 8:
                i, t = u // 2, 1 - u % 2
                heads = [g * A_PER + i for g in range(A_GROUPS)]
                w = S if t else P
                return dict(t=t, w=w, n=3, low=[x % 2 for x in heads], joint=True, par=u % 2, slot=u % 4, probs=u % 2 * 768, one_bank=False, scale=SCALE,
                            q=[qa[64 * (x % 2):64 * (x % 2) + 64, x // 2, t * P:(t + 1) * P] for x in heads],
                            k=[ka[64 * (x % 2):64 * (x % 2) + 64, x // 2, 0:w] for x in heads],
                            v=[[va[:, kt, x * HD:(x + 1) * HD] for kt in range(w // P)] for x in heads],
                            bias=bias_a[:, :, i, S - w:S], out=o_a[:, t, i * HD:(i + 1) * HD])
            c = u - 8
            t, heads = (1, [2 * c, 2 * c + 1]) if c < 4 else (0, list(range(4 * (c - 4), 4 * (c - 4) + 4)))
            w = S if t else P
            return dict(t=t, w=w, n=len(heads), low=[x % 2 for x in heads], joint=False, par=u % 2, slot=u % 4, probs=u % 2 * 768, one_bank=False, scale=SCALE,
                        q=[qc[64 * (x % 2):64 * (x % 2) + 64, x // 2, t * P:(t + 1) * P] for x in heads],
                        k=[kc[64 * (x % 2):64 * (x % 2) + 64, x // 2, 0:w] for x in heads],
                        v=[[vc[:, kt, x * HD:(x + 1) * HD] for kt in range(w // P)] for x in heads],
                        bias=bias_c[:, heads[0]:heads[-1] + 1, S - w:S],
                        out=o_c[:, t, heads[0] * HD:(heads[-1] + 1) * HD])

        def unit_layer(i):
            kind = "A" if i < 6 else "C" if i < 9 else "B"
            c = i if kind == "A" else (i - 6) % 3
            late = 4 if kind == "A" else 2
            t, heads = (1, [2 * c, 2 * c + 1]) if c < late else (0, list(range(4 * (c - late), 4 * (c - late) + 4)))
            w = S if t else P
            x0, x1 = heads[0], heads[-1] + 1
            if kind == "A":
                q = [aq_t[64 * (x % 2):64 * (x % 2) + 64, x // 2, t * P:(t + 1) * P] for x in heads]
                k = [ak_t[64 * (x % 2):64 * (x % 2) + 64, x // 4, 0:w] for x in heads]
                v = [[h[:, kt, AV + (x // 4) * HD:AV + (x // 4 + 1) * HD] for kt in range(w // P)] for x in heads]
                bias, o = cst[:, C_MA + S - w:C_MA + S], x0 * HD
            elif kind == "C":
                q = [qc_t[0:96, x, t * P:(t + 1) * P] for x in heads]
                k = [kc_t[0:96, x, 0:w] for x in heads]
                v = [[kv_c[:, kt, x * 128 + 64:x * 128 + 128] for kt in range(w // P)] for x in heads]
                bias, o = cst[:, C_MC + S - w:C_MC + S], 768 + x0 * HD
            else:
                q = [bq_t[64 * (x % 2):64 * (x % 2) + 64, x // 2, t * P:(t + 1) * P] for x in heads]
                k = [bk_t[64 * (x % 2):64 * (x % 2) + 64, 0:w] for x in heads]
                v = [[h[:, kt, BV:BV + HD] for kt in range(w // P)] for x in heads]
                bias, o = mask_b[:, 0:256] if t else mask_b[:, 256:384], 512 + x0 * HD
            return dict(t=t, w=w, n=len(heads), low=[kind != "C" and x % 2 for x in heads], joint=False, par=i % 2, slot=i % 4, probs=i % 3 * 512, one_bank=True, kind=kind, heads=(x0, x1),
                        scale=C2_SCALE if kind == "C" else SCALE, q=q, k=k, v=v, bias=spread(bias, 1, len(heads)),
                        out=mix_tok[:, t, o:o + (x1 - x0) * HD])

        def scores_at(u):
            a = 4 + u["par"] if u["one_bank"] else 4
            n = u["n"] * u["w"]
            return banks(a, a + (1 if n <= 512 else 2))[:, 0:n].rearrange("p (n w) -> p n w", w=u["w"])

        def probs_at(u):
            return pbuf.rearrange("p a b -> p (a b)")[:, u["probs"]:u["probs"] + u["n"] * u["w"]]\
                .rearrange("p (n w) -> p n w", w=u["w"])

        def pv_at(u):
            return ps[:, 6 + u["par"], 0:HD if u["joint"] else u["n"] * HD]

        @block.sync
        def _(sp):
            def load(c, v, n, src):
                if not isinstance(v, int):
                    apart(sp, hi_made, v * 3 + (c - 2))
                    sp.wait_ge(lo_made, v * 3 + (c - 2))
                elif c + 3 * v >= 3:
                    sp.wait_ge(hi_made, v * 3 + (c - 2))
                    sp.wait_ge(lo_made, v * 3 + (c - 2))
                d = raw[:, c % 3, 0:n]
                if len(src.shape) == 3:
                    d = d.rearrange("p (a b) -> p a b", a=src.shape[1])
                sp.dma_start(d, src).then_inc(raw_in[c % 3], 16)

            w_in = I["w_in"][0].rearrange("(k p) c -> p k c", p=P)
            sp.dma_start(x_tok[:, :, :], I["x"][0].rearrange("(t p) d -> p t d", p=P)).then_inc(x_in, 16)
            for n, tile in enumerate(COL_TILES):
                load(n, 0, TW, w_in[:, :, tile * 256:(tile + 1) * 256])
            load(T_PA, 0, TW, I["p_a"][0].rearrange("(k p) c -> p k c", p=P))
            for j in range(2):
                load(T_PB + j, 0, TW, I["p_b"][0].rearrange("(k p) c -> p k c", p=P)[:, :, j * 512:(j + 1) * 512])
            for j in range(2):
                load(T_PC + j, 0, TW, I["p_c"][0].rearrange("(k p) c -> p k c", p=P)[:, :, j * 512:(j + 1) * 512])
            sp.wait_ge(o_ready, 14)
            sp.dma_start(g_ffn, rows_of(I["g_ffn"][0])).then_inc(g_in, 16)
            for j in range(4):
                load(T_WO + j, 0, TW, I["w_out"][0].rearrange("(a k p) c -> a p k c", k=2, p=P)[j])
            sp.wait_ge(hb_lo, 1)
            sp.dma_start(g_fin, rows_of(I["g_final"])).then_inc(g_in, 16)
            w_gu = I["w_gu"][0].rearrange("(k p) c -> p k c", p=P)
            w_dn = I["w_down"][0].rearrange("(a k p) c -> a p k c", k=2, p=P)
            load(T_FFN, 0, TW, w_gu[:, :, 0:256])
            load(T_FFN + 1, 0, TW, w_gu[:, :, FFN:FFN + 256])
            with sp.Fori(1, FFN_E) as e:
                load(T_FFN - 1, e, TW, w_gu[:, :, bass.ds(e * 256, 256)])
                load(T_FFN, e, TW, w_gu[:, :, bass.ds(e * 256 + FFN, 256)])
                load(T_FFN + 1, e, TW, w_dn[e - 1])
            load(T_FFN + 3 * FFN_E - 1, 0, TW, w_dn[FFN_E - 1])

            w_in2 = I["w_in_2"].rearrange("l (k p) c -> l p k c", p=P)
            w_uq = I["w_uq_2"].rearrange("l (k p) c -> l p k c", p=P)
            w_o2 = I["w_out_2"].rearrange("l (a k p) c -> (l a) p k c", k=2, p=P)
            w_rt = I["w_router_2"].rearrange("(k p) c -> p k c", p=P)
            w_g = I["w_gate_2"].rearrange("l e (k p) c -> (l e) p k c", p=P)
            w_u = I["w_up_2"].rearrange("l e (k p) c -> (l e) p k c", p=P)
            w_d = I["w_down_2"].rearrange("l e (k p) c -> (l e) p k c", p=P)
            with sp.Fori(0, LAYERS) as l:
                for j, tile in enumerate(L_COLS):
                    n = min(256, IN2 - tile * 256)
                    load(T_L + j, l * 21, KD * n, w_in2[l, :, :, tile * 256:tile * 256 + n])
                load(T_L + J_UQ, l * 21, 768, w_uq[l])
                load(T_L + J_UKV, l * 21, 512, I["w_ukv_2"][l])
                for j in range(4):
                    load(T_L + J_WO + j, l * 21, TW, w_o2[l * 4 + j])
                load(T_L + J_RT, l * 21, 128, w_rt)
                apart(sp, o_ready, l * U_PER + (U_L0 + U_PER))
                sp.dma_start(ln_g, rows_of(I["ln1_g_2"][l])).then_inc(gln_in, 16)
                sp.dma_start(ln_b, rows_of(I["ln1_b_2"][l])).then_inc(gln_in, 16)
                load(T_L + J_MOE, l * 21, TW, w_g[l * N_EXP])
                load(T_L + J_MOE + 1, l * 21, TW, w_u[l * N_EXP])
                apart(sp, tok_ready, l * 4 + 8)
                sp.dma_start(ln_g, rows_of(I["ln2_g_2"][l])).then_inc(gln_in, 16)
                sp.dma_start(ln_b, rows_of(I["ln2_b_2"][l])).then_inc(gln_in, 16)
                with sp.Fori(1, N_EXP) as e:
                    load(T_L + J_MOE - 1, l * 21 + e, TW, w_g[l * N_EXP + e])
                    load(T_L + J_MOE, l * 21 + e, TW, w_u[l * N_EXP + e])
                    load(T_L + J_MOE + 1, l * 21 + e, TW, w_d[l * N_EXP + e - 1])
                load(T_L + L_TILES - 1, l * 21, TW, w_d[l * N_EXP + (N_EXP - 1)])
            sp.wait_ge(tok_ready, 6 + 4 * LAYERS)
            sp.dma_start(out[0].rearrange("(t p) d -> p t d", p=P), x_tok[:, :, :]).then_inc(out_done, 16)
            sp.wait_ge(out_done, 16)

        @block.gpsimd
        def _(pool):
            link = Chain(pool, pool_seq)
            pool.dma_start(ident, I["shape_consts"][:, 0:P]).then_inc(c_in, 16)
            pool.dma_start(g_mix, rows_of(I["g_mix"][0])).then_inc(gmix_in, 16)
            pool.dma_start(buck, I["shape_buckets"]).then_inc(init_in, 16)
            pool.dma_start(tabx[0:32, :], I["rel_bias"]).then_inc(init_in, 16)
            pool.dma_start(tabx[32:36, :], I["shape_groups"]).then_inc(init_in, 16)
            pool.dma_start(prm[0:4, :], I["conv_w"][0]).then_inc(prm_in, 16)
            for i, name in enumerate(("conv_b", "lru_ba", "lru_bx", "lru_lam")):
                pool.dma_start(prm[4 + i:5 + i, :], I[name]).then_inc(prm_in, 16)
            pool.memset(mhalf[:, :], -0.5).then_inc(mhalf_set, 1)
            pool.wait_ge(mhalf_set, 1)
            pool.memset(bd_a[:, :, :], 0.0).then_inc(bd_zero, 1)
            pool.memset(bd_x[:, :, :], 0.0).then_inc(bd_zero, 1)
            pool.wait_ge(bd_zero, 2)
            for bd, name in ((bd_a, "lru_wa"), (bd_x, "lru_wx")):
                src = I[name][0].rearrange("(c two) d e -> two d c e", two=2)
                for half in range(2):
                    a = 64 * half
                    pool.dma_start(bd[a:a + 64, :, a:a + 64], src[half]).then_inc(lru_in, 16)

            def power(var_n, n):
                pool.wait_ge(var_ready, var_n + 1)
                t = n
                pool.tensor_tensor(rstd[:, t:t + 1], var[:, t:t + 1], mhalf[:, 0:1], ALU.pow).then_inc(rstd_ready, 1)

            power(0, 0)
            power(1, 1)
            pool.wait_ge(ext_sb, 1)
            pool.dma_start(bias_dram.ap(), ext).then_inc(ext_out, 16)
            pool.wait_ge(ext_out, 16)
            rows = bias_dram.ap()
            src = bass.AP(rows.tensor, 0, [[1, P], [2 * S, A_HEADS], [1, S]])
            pool.dma_start(bias_a.rearrange("p g i w -> p (g i) w"), src).then_inc(bias_in, 16)
            src = bass.AP(rows.tensor, A_HEADS * 2 * S, [[1, P], [2 * S, C_HEADS], [1, S]])
            pool.dma_start(bias_c, src).then_inc(bias_in, 16)
            pool.wait_ge(tr_full, 4)
            pool.memset(xbp[:, :, 0:3], 0.0).then_inc(pad_zero, 1)
            pool.wait_ge(lru_full, 1)
            pool.dma_start(cst[:, P:C_ALL], I["shape_consts"][:, P:C_ALL]).then_inc(c2_in, 16)
            pool.wait_ge(ring_free, 13)
            pool.wait_ge(o_ready, 8)
            g2 = gb.rearrange("p a b -> p (a b)")
            link(pool.tensor_tensor(gelu_t, g2, g2, ALU.mult))
            link(pool.tensor_scalar(gelu_t, gelu_t, 0.044715, 1.0, ALU.mult, ALU.add))
            pool.tensor_tensor(gelu_t, gelu_t, g2, ALU.mult).then_inc(gelu_in, 1)
            pool.wait_ge(gelu_tanh, 1)
            link(pool.tensor_scalar(gelu_t, gelu_t, 1.0, 0.5, ALU.add, ALU.mult))
            pool.tensor_tensor(g2, g2, gelu_t, ALU.mult).then_inc(gelu_done, 1)
            for n in range(2, 6):
                power(n, n % 2)
            pool.wait_ge(c2_in, 16)

            with pool.Fori(0, LAYERS) as l:
                lk = Chain(pool, pool_seq_l, 0, POOL_LINKS, l)

                def rope(heads, dim, cc, ss, src, last, keys=()):
                    for t in range(TT):
                        x = src(t)
                        n = heads * dim
                        a3 = rope_a[:, 0:n].rearrange("p (h d) -> p h d", d=dim)
                        b3 = rope_b[:, 0:n].rearrange("p (h d) -> p h d", d=dim)
                        c3 = spread(cst[:, cc + t * dim:cc + (t + 1) * dim], 1, heads)
                        half = dim // 2
                        s_lo = spread(cst[:, ss + t * dim:ss + t * dim + half], 1, heads)
                        s_hi = spread(cst[:, ss + t * dim + half:ss + (t + 1) * dim], 1, heads)
                        pool.tensor_tensor(a3, x, c3, ALU.mult)
                        pool.tensor_tensor(b3[:, :, 0:half], x[:, :, half:dim], s_lo, ALU.mult)
                        lk(pool.tensor_tensor(b3[:, :, half:dim], x[:, :, 0:half], s_hi, ALU.mult))
                        ins = pool.tensor_tensor(x, a3, b3, ALU.add)
                        if t == TT - 1 and last and not keys:
                            ins.then_inc(rope_done, 1)
                            pool.wait_ge(rope_done, l * 4 + last)
                        else:
                            lk(ins, apart if t == TT - 1 else None)
                    for which, c0 in keys:
                        for t in range(TT):
                            ins = pool.tensor_copy(twice[which][:, t, :].rearrange("p (a d) -> p a d", a=2),
                                                   spread(h[:, t, c0:c0 + 64], 1, 2))
                    if keys:
                        ins.then_inc(rope_done, 1)

                def cols(c0, heads, dim=64):
                    return lambda t: h[:, t, c0:c0 + heads * dim].rearrange("p (h d) -> p h d", d=dim)

                pool.wait_ge(ring_free, l * 8 + (N_COL + 3))
                rope(10, 64, C_CC, C_SS, cols(AQ, 10), 1, [(2, AK), (3, AK + 64)])
                pool.wait_ge(ring_free, l * 8 + (N_COL + 5))
                rope(5, 64, C_CC, C_SS, cols(IQ, 5), 2, [(0, IK)])
                pool.wait_ge(ring_free, l * 8 + (N_COL + 7))
                rope(1, 32, C_CC16, C_SS16, cols(CKR, 1, 32), 3)
                pool.wait_ge(cn_var, l + 1)
                pool.tensor_tensor(crstd[:, :], cvar[:, :], mhalf[:, :], ALU.pow).then_inc(cn_rstd, 1)
                pool.wait_ge(ring_free, l * 8 + (N_COL + 8))
                rope(5, 64, C_CC, C_SS, cols(BQ, 5), 4, [(1, BK)])
                pool.wait_ge(ukv_sb, l * 4 + 4)
                rope(4, 32, C_CC16, C_SS16,
                     lambda t: q_c[:, t, :].rearrange("p (h d) -> p h d", d=96)[:, :, 64:96], 0)
                for t in range(TT):
                    kn = kv_c[:, t, :].rearrange("p (h d) -> p h d", d=128)[:, :, 0:64]
                    pool.tensor_copy(kcat[:, t, :, 0:64], kn)
                    ins = pool.tensor_copy(kcat[:, t, :, 64:96], spread(h[:, t, CKR:CKR + 32], 1, 4))
                ins.then_inc(kcat_ready, 1)
                for t in range(TT):
                    power(l * 4 + (6 + t), t)
                apart(pool, gt_ready, l + 1)
                pool.dma_start(gate_dram.ap(), gt_sb).then_inc(gt_out, 16)
                apart(pool, gt_out, l * 16 + 16)
                flat = bass.AP(gate_dram.ap().tensor, 0, [[0, P], [1, N_EXP * S]])
                pool.dma_start(gate_bc.rearrange("p a b -> p (a b)"), flat).then_inc(gate_in, 16)
                for t in range(TT):
                    power(l * 4 + (8 + t), t)
                assert lk.n == POOL_LINKS, lk.n

        @block.tensor
        def _(pe):
            link = Chain(pe, pe_seq)

            def tile_ready(c, v=0):
                pe.wait_ge(lo_made, v * 3 + (c + 1))

            def three(o, ah, al, bh, bl, first, last):
                pe.matmul(o, ah, bh, start=first, stop=False)
                pe.matmul(o, ah, bl, start=False, stop=False)
                return pe.matmul(o, al, bh, start=False, stop=last)

            def cols_tile(c, v, bank, n, rows, parts=(0, 1)):
                tile_ready(c, v)
                s = c % 3
                wh = whi[:, s, 0:KD * n].rearrange("p (k c) -> p k c", k=KD)
                wl = wlo[:, s, 0:KD * n].rearrange("p (k c) -> p k c", k=KD)
                for part in parts:
                    m = slice(part * P, (part + 1) * P)
                    for k in range(KD):
                        f, g = k == 0, k == KD - 1
                        if rows:
                            o = ps[:, bank, part * 256:part * 256 + n]
                            last = three(o, act_hi[:, k, m], act_lo[:, k, m], wh[:, k, :], wl[:, k, :], f, g)
                        else:
                            o = ps[:, bank, part * 256:(part + 1) * 256]
                            last = three(o, wh[:, k, m], wl[:, k, m], act_hi[:, k, :], act_lo[:, k, :], f, g)
                if parts[-1] == 1:
                    last.then_inc(tile_used, 1)

            def down_tile(c, v, hi, lo, first, last):
                tile_ready(c, v)
                s = c % 3
                wh = whi[:, s, :].rearrange("p (k c) -> p k c", k=2)
                wl = wlo[:, s, :].rearrange("p (k c) -> p k c", k=2)
                for t in range(TT):
                    for half in range(2):
                        for k in range(2):
                            m, n = slice(t * P, (t + 1) * P), slice(half * 512, half * 512 + 512)
                            o = ps[:, 4 + 2 * t + half, :]
                            f, g = first and k == 0, last and k == 1
                            a, b, cc, d = hi[:, k, m], lo[:, k, m], wh[:, k, n], wl[:, k, n]
                            pe.matmul(o, a, cc, start=f, stop=False)
                            pe.matmul(o, a, d, start=False, stop=False)
                            x = pe.matmul(o, b, cc, start=False, stop=g)
                    if last and t == 0:
                        x.then_inc(early_out, 1)
                x.then_inc(tile_used, 1)

            def turn(src, t):
                for half in range(2):
                    for i in range(4):
                        k = 4 * half + i
                        x = pe.transpose(ps[:, 2 * t + half, i * P:(i + 1) * P], src[:, t, k * P:(k + 1) * P], ident)
                    x.then_inc(tr_full, 1)

            def scores(u, n, lk):
                pe.wait_ge(l_ready, n - 1 if u["one_bank"] else n) if not (isinstance(n, int) and n == 0) else None
                o, low = scores_at(u), None
                for i in sorted(range(u["n"]), key=lambda i: u["low"][i]):
                    if low is not None and u["low"][i] != low:
                        lk(x)
                    low = u["low"][i]
                    x = pe.matmul(o[:, i, :], u["q"][i], u["k"][i], start=True, stop=True)
                x.then_inc(sc_full, 1)

            def turn_probs(u, n):
                pe.wait_ge(p_ready, n + 1)
                if not (isinstance(n, int) and n == 0):
                    pe.wait_ge(pt_ready, n)
                p, w = probs_at(u), u["w"]
                o = banks(2, 4)
                for i in range(u["n"]):
                    for kt in range(w // P):
                        b = i * (w // P) + kt
                        x = pe.transpose(o[:, b * P:(b + 1) * P], p[:, i, kt * P:(kt + 1) * P], ident)
                x.then_inc(pt_full, 1)

            def values(u, n):
                pe.wait_ge(pt_ready, n + 1)
                if not (isinstance(n, int) and n < 2):
                    pe.wait_ge(o_ready, n - 1)
                o, kts = pv_at(u), u["w"] // P
                for i in range(u["n"]):
                    for kt in range(kts):
                        b = i * kts + kt
                        if u["joint"]:
                            oo, f, g = o, b == 0, b == u["n"] * kts - 1
                        else:
                            oo, f, g = o[:, i * HD:(i + 1) * HD], kt == 0, kt == kts - 1
                        x = pe.matmul(oo, pt[:, b * P:(b + 1) * P], u["v"][i][kt], start=f, stop=g)
                x.then_inc(pv_full, 1)

            pe.wait_ge(init_in, 48)
            pe.matmul(ps[0:20, 7, :], tabx[:, :], buck, start=True, stop=True).then_inc(ext_full, 1)
            pe.wait_ge(prm_in, 80)
            pe.wait_ge(c_in, 16)
            for c in range(LC):
                x = pe.transpose(ps[:, 6, c * 8:(c + 1) * 8], prm[:, c * P:(c + 1) * P], ident[0:8, 0:8])
            x.then_inc(prm_full, 1)
            for t in range(TT):
                pe.wait_ge(tok_ready, t + 1)
                turn(xn1, t)
            pe.wait_ge(tr_lo, 4)
            for s in range(N_COL):
                if s == 9:
                    pe.wait_ge(ext_sb, 1)
                    pe.wait_ge(prm_sb, 1)
                if 9 <= s < 17:
                    pe.wait_ge(ring_free, 9)
                    scores(unit_first(s - 9), s - 9, link)
                if 19 <= s < 25:
                    pe.wait_ge(ring_free, 17)
                    pe.wait_ge(lru_gates, 2)
                    scores(unit_first(8 + s - 19), 8 + s - 19, link)
                if s >= 2:
                    pe.wait_ge(ring_free, s - 1)
                rows = COL_TILES[s] in (6, 7, 8, 17, 18)
                cols_tile(s, 0, s % 2, 256, rows)
                if 9 <= s < 17:
                    turn_probs(unit_first(s - 9), s - 9)
                if 10 <= s < 18:
                    values(unit_first(s - 10), s - 10)
                if s == 18:
                    pe.wait_ge(xc_ready, 1)
                    pe.wait_ge(lru_in, 64)
                    pe.wait_ge(l_ready, 8)
                    pe.wait_ge(pt_ready, 8)
                    for b0, bd in ((4, bd_a), (2, bd_x)):
                        for c in range(LC):
                            o = ps[:, b0 + c // 2, (c % 2) * 256:(c % 2) * 256 + 256]
                            x = pe.matmul(o, bd[:, c, :], xc[:, c, :], start=True, stop=True)
                    x.then_inc(lru_full, 1)
                if 19 <= s < 25:
                    turn_probs(unit_first(8 + s - 19), 8 + s - 19)
                if 20 <= s < 26:
                    values(unit_first(8 + s - 20), 8 + s - 20)
                if s == 28:
                    pe.wait_ge(o_ready, 14)
                    pe.wait_ge(pt_ready, 14)
                    for q in range(6):
                        src = o_a[:, :, q * P:(q + 1) * P] if q < 2 else o_c[:, :, (q - 2) * P:(q - 1) * P]
                        for t in range(TT):
                            b = 2 * q + t
                            x = pe.transpose(ps[:, (2, 3, 6)[b // 4], (b % 4) * P:(b % 4 + 1) * P], src[:, t, :], ident)
                    x.then_inc(ot_full, 1)

            def project(c, banks_, kk, k0):
                tile_ready(c)
                w = TW // kk
                wh = whi[:, c % 3, :].rearrange("p (k c) -> p k c", k=kk)
                wl = wlo[:, c % 3, :].rearrange("p (k c) -> p k c", k=kk)
                for ct in range(w // P):
                    o = ps[:, banks_[ct // 2], (ct % 2) * 256:(ct % 2) * 256 + 256]
                    m = slice(ct * P, (ct + 1) * P)
                    for k in range(kk):
                        x = three(o, wh[:, k, m], wl[:, k, m], mix_hi[:, k0 + k, :], mix_lo[:, k0 + k, :], k == 0, k == kk - 1)
                x.then_inc(tile_used, 1)

            pe.wait_ge(ring_free, N_COL)
            pe.wait_ge(ot_lo, 3)
            project(T_PA, (0, 1, 2, 3), 2, 0)
            pe.wait_ge(hb_lo, 1)
            project(T_PB, (4, 5), 4, 2)
            project(T_PB + 1, (6, 7), 4, 2)
            pe.wait_ge(p_read, 1)
            project(T_PC, (0, 1), 4, 6)
            project(T_PC + 1, (2, 3), 4, 6)
            pe.wait_ge(p_read, 3)
            for j in range(4):
                pe.wait_ge(m_lo, j // 2 + 1)
                down_tile(T_WO + j, 0, act_hi[:, 2 * j:2 * j + 2, :], act_lo[:, 2 * j:2 * j + 2, :], j == 0, j == 3)
            for t in range(TT):
                pe.wait_ge(tok_ready, 3 + t)
                pe.wait_ge(p_read, 5)
                turn(xn2, t)

            def experts(c0, v0, count, done0, hot):
                def gate_up(c, v, e, between=None):
                    first = isinstance(done0, int) and isinstance(e, int) and done0 + e == 0
                    if not first:
                        pe.wait_ge(silu_done, done0 + e)
                    cols_tile(c, v, 0, 256, False)
                    if between:
                        between()
                    if not first:
                        pe.wait_ge(t_ready, done0 + e)
                    cols_tile(c + 1, v, 1, 256, False)

                def down(c, v, e, first, last):
                    pe.wait_ge(hid_l, done0 + e)
                    down_tile(c, v, hid_hi, hid_lo, first, last)

                gate_up(c0, v0, 0, hot)
                gate_up(c0 - 1, v0 + 1, 1)
                down(c0 + 1, v0 + 1, 1, True, False)
                with pe.Fori(2, count) as e:
                    gate_up(c0 - 1, v0 + e, e)
                    down(c0 + 1, v0 + e, e, False, False)
                down(c0 + 3 * count - 1, v0, count, False, True)

            pe.wait_ge(tr_lo, 8)
            experts(T_FFN, 0, FFN_E, 0, None)

            with pe.Fori(0, LAYERS) as l:
                v = l * 21
                lk = Chain(pe, pe_seq_l, 0, PE_LINKS, l)
                for t in range(TT):
                    pe.wait_ge(tok_ready, l * 4 + (5 + t))
                    turn(x_tok, t)
                    if t == 0:
                        pe.wait_ge(tr_lo, l * 12 + 10)
                        cols_tile(T_L, v, N_COL % 2, L_WIDTHS[0], True, (0,))
                cols_tile(T_L + 1, v, (N_COL + 1) % 2, L_WIDTHS[1], True, (0,))
                pe.wait_ge(tr_lo, l * 12 + 12)

                def turns(items, k=P):
                    for b, src in enumerate(items):
                        x = pe.transpose(banks(2, 4)[0:k, b * P:(b + 1) * P], src, ident)
                    x.then_inc(tb_full, 1)

                def tb_wait(b):
                    pe.wait_ge(tb_free, l * 6 + b)

                def pairs(c0, n):
                    return [h[:, t, c0 + i * P:c0 + (i + 1) * P] for i in range(n) for t in range(TT)]

                def doubled(which):
                    return [twice[which][:, t, :] for t in range(TT)]

                for j in range(8):
                    if j >= 2:
                        pe.wait_ge(ring_free, l * 8 + (N_COL + j - 1))
                    cols_tile(T_L + j, v, (N_COL + j) % 2, L_WIDTHS[j], True, (1,) if j < 2 else (0, 1))
                    if j == 5:
                        pe.wait_ge(rope_done, l * 4 + 1)
                        turns(pairs(AQ, 3))
                    if j == 6:
                        tb_wait(1)
                        turns([h[:, t, AQ + 384:AQ + 512] for t in range(TT)] + doubled(2) + doubled(3))
                pe.wait_ge(rope_done, l * 4 + 2)
                tb_wait(2)
                turns(pairs(IQ, 2) + doubled(0))
                tb_wait(3)
                for t, o, w in ((1, banks(4, 6), S), (0, banks(6, 7), P)):
                    for x in (0, 2, 1, 3):
                        a = 64 * (x % 2)
                        if x == 1:
                            lk(ins)
                        ins = pe.matmul(o[:, x * w:(x + 1) * w], iq_t[a:a + 64, x // 2, t * P:(t + 1) * P],
                                        ik_t[a:a + 64, 0:w], start=True, stop=True)
                ins.then_inc(idx_full, 1)

                def up_queries():
                    pe.wait_ge(ring_free, l * 8 + (N_COL + 8))
                    tile_ready(T_L + J_UQ, v)
                    s = (T_L + J_UQ) % 3
                    wh = whi[:, s, 0:768].rearrange("p (k c) -> p k c", k=2)
                    wl = wlo[:, s, 0:768].rearrange("p (k c) -> p k c", k=2)
                    for t in range(TT):
                        m = slice(t * P, (t + 1) * P)
                        for k in range(2):
                            x = three(ps[:, t, 0:384], mix_hi[:, k, m], mix_lo[:, k, m], wh[:, k, :], wl[:, k, :], k == 0, k == 1)
                    x.then_inc(tile_used, 1)

                def up_keys():
                    tile_ready(T_L + J_UKV, v)
                    s = (T_L + J_UKV) % 3
                    pe.wait_ge(ukv_sb, l * 4 + 2)
                    for t in range(TT):
                        m = slice(t * P, (t + 1) * P)
                        x = three(ps[:, t, :], mix_hi[:, 2, m], mix_lo[:, 2, m], whi[:, s, 0:512], wlo[:, s, 0:512], True, True)
                    x.then_inc(tile_used, 1)

                pe.wait_ge(idx_relu, l + 1)
                nu = l * U_PER + U_L0
                for i in range(U_PER + 3):
                    if i == 1:
                        pe.wait_ge(cn_ready, l + 1)
                        turns([cn[:, t, q * P:(q + 1) * P] for q in range(3) for t in range(TT)])
                    if i == 2:
                        pe.wait_ge(cn_lo, l + 1)
                        up_queries()
                    if i == 3:
                        up_keys()
                    if i in (5, 6, 8):
                        pe.wait_ge(pt_ready, nu + (i - 2))
                    if i == 5:
                        pe.wait_ge(kcat_ready, l + 1)
                        turns([q_c[:, t, x * 96:(x + 1) * 96] for x in range(4) for t in range(TT)], 96)
                    if i == 6:
                        turns([kcat[:, t, x, :] for x in range(4) for t in range(TT)], 96)
                        tb_wait(5)
                    if i == 8:
                        pe.wait_ge(rope_done, l * 4 + 4)
                        turns(pairs(BQ, 2) + doubled(1))
                    if i < U_PER:
                        scores(unit_layer(i), nu + i, lk)
                    if i in (5, 8):
                        tb_wait({5: 4, 8: 6}[i])
                    if 2 <= i < U_PER + 2:
                        turn_probs(unit_layer(i - 2), nu + (i - 2))
                    if i >= 3:
                        values(unit_layer(i - 3), nu + (i - 3))
                pe.wait_ge(o_ready, nu + U_PER)
                for t in range(TT):
                    turn(mix_tok, t)
                for j in range(4):
                    pe.wait_ge(tr_lo, l * 12 + 16)
                    down_tile(T_L + J_WO + j, v, mix_hi[:, 2 * j:2 * j + 2, :], mix_lo[:, 2 * j:2 * j + 2, :], j == 0, j == 3)
                for t in range(TT):
                    pe.wait_ge(tok_ready, l * 4 + (7 + t))
                    turn(x_tok, t)
                pe.wait_ge(tr_lo, l * 12 + 20)
                tile_ready(T_L + J_RT, v)
                s = (T_L + J_RT) % 3
                wh = whi[:, s, 0:128].rearrange("p (k c) -> p k c", k=KD)
                wl = wlo[:, s, 0:128].rearrange("p (k c) -> p k c", k=KD)
                for t in range(TT):
                    m = slice(t * P, (t + 1) * P)
                    for k in range(KD):
                        x = three(ps[:, 2, t * 16:(t + 1) * 16], act_hi[:, k, m], act_lo[:, k, m], wh[:, k, :], wl[:, k, :],
                                  k == 0, k == KD - 1)
                x.then_inc(tile_used, 1)

                def gate_rows():
                    pe.wait_ge(gts_ready, l + 1)
                    for t in range(TT):
                        x = pe.transpose(ps[0:16, 3, t * P:(t + 1) * P], rt[2][:, t, :], ident)
                    x.then_inc(gt_full, 1)

                experts(T_L + J_MOE, v, N_EXP, l * N_EXP + FFN_E, gate_rows)
                assert lk.n == PE_LINKS

        @block.scalar
        def _(act):
            link = Chain(act, act_seq)

            def split_hi(c, v=0, n=TW):
                act.wait_ge(raw_in[c % 3], v * 16 + 16 * (c // 3 + 1))
                if not (isinstance(v, int) and c + 3 * v < 3):
                    act.wait_ge(tile_used, v * 3 + (c - 2))
                act.activation(whi[:, c % 3, 0:n], raw[:, c % 3, 0:n], ACT.Copy).then_inc(hi_made, 1)

            def turned_hi(n, dst):
                for t in range(TT):
                    for half in range(2):
                        act.wait_ge(tr_full, n * 4 + (2 * t + half + 1))
                        act.activation(dst[:, 4 * half:4 * half + 4, t * P:(t + 1) * P],
                                       ps[:, 2 * t + half, :].rearrange("p (k c) -> p k c", k=4), ACT.Copy).then_inc(tr_hi, 1)

            def exps(u, n):
                act.wait_ge(l_ready, n + 1)
                p = probs_at(u)
                if u["joint"]:
                    x = act.activation(p, p, ACT.Exp, bias=negm[:, u["slot"], 0:1], accum_out=den[:, u["slot"], 0:1])
                else:
                    for i in range(u["n"]):
                        x = act.activation(p[:, i, :], p[:, i, :], ACT.Exp, bias=negm[:, u["slot"], i:i + 1],
                                           accum_out=den[:, u["slot"], i:i + 1])
                if u.get("kind") == "A":
                    act.activation(esink[:, u["slot"], 0:u["n"]], esink[:, u["slot"], 0:u["n"]], ACT.Exp)\
                        .then_inc(p_ready, 1)
                else:
                    x.then_inc(p_ready, 1)

            def probs_out(u, n):
                act.wait_ge(pt_full, n + 1)
                if not (isinstance(n, int) and n == 0):
                    act.wait_ge(pv_full, n)
                m = u["n"] * u["w"]
                act.activation(pt[:, 0:m], banks(2, 4)[:, 0:m], ACT.Copy).then_inc(pt_ready, 1)

            split_hi(0)
            split_hi(1)
            act.wait_ge(lam_abs, 1)
            act.activation(lam[:, 1, :], lam[:, 0, :], ACT.Exp, scale=-1.0).then_inc(lam_exp, 1)
            act.wait_ge(ext_full, 1)
            act.activation(ext, ps[0:20, 7, :], ACT.Copy).then_inc(ext_sb, 1)
            turned_hi(0, act_hi)

            def evac(s):
                act.wait_ge(tile_used, s + 1)
                ct = COL_TILES[s]
                src = ps[:, s % 2, :].rearrange("p (a b) -> p a b", a=2)
                if ct < 3:
                    dst = qa[:, 2 * ct:2 * ct + 2, :]
                elif ct < 6:
                    dst = ka[:, 2 * (ct - 3):2 * (ct - 3) + 2, :]
                elif ct < 9:
                    dst = va[:, :, (ct - 6) * 256:(ct - 5) * 256]
                elif ct < 11:
                    if ct == 9:
                        act.wait_ge(pad_zero, 1)
                        act.wait_ge(tr_lo, 4)
                    dst = xbp[:, 2 * (ct - 9):2 * (ct - 9) + 2, 3:3 + S]
                elif ct < 13:
                    dst = gb[:, 2 * (ct - 11):2 * (ct - 11) + 2, :]
                elif ct < 15:
                    dst = qc[:, 2 * (ct - 13):2 * (ct - 13) + 2, :]
                elif ct < 17:
                    dst = kc[:, 2 * (ct - 15):2 * (ct - 15) + 2, :]
                elif ct < 19:
                    dst = vc[:, :, (ct - 17) * 256:(ct - 16) * 256]
                else:
                    if ct == 19:
                        act.wait_ge(pv_full, 8)
                    act.activation(gates[:, 2 * (ct - 19):2 * (ct - 19) + 2, :], src, ACT.Copy if s < G_LATE else ACT.Sigmoid)\
                        .then_inc(ring_free, 1)
                    return
                if ct < 3 or 13 <= ct < 15:
                    dst = dst.rearrange("p a (t q) -> p (a t) q", q=P)
                    src = backward(src.rearrange("p a (t q) -> p (a t) q", q=P))
                act.activation(dst, src, ACT.Copy).then_inc(ring_free, 1)

            for s in range(N_COL):
                if 10 <= s < 18:
                    probs_out(unit_first(s - 10), s - 10)
                if 20 <= s < 26:
                    probs_out(unit_first(8 + s - 20), 8 + s - 20)
                if s >= 1:
                    evac(s - 1)
                if 9 <= s < 17:
                    exps(unit_first(s - 9), s - 9)
                if s == 19:
                    act.wait_ge(lru_full, 1)
                    act.wait_ge(prm_sb, 1)
                    for c in range(LC):
                        x = act.activation(rr[:, c, :], ps[:, 4 + c // 2, (c % 2) * 256:(c % 2) * 256 + 256], ACT.Sigmoid,
                                           bias=prm_t[:, c, 5:5+1])
                    x.then_inc(lru_gates, 1)
                    for c in range(LC):
                        x = act.activation(ig[:, c, :], ps[:, 2 + c // 2, (c % 2) * 256:(c % 2) * 256 + 256], ACT.Sigmoid,
                                           bias=prm_t[:, c, 6:6+1])
                    x.then_inc(lru_gates, 1)
                if 19 <= s < 25:
                    exps(unit_first(8 + s - 19), 8 + s - 19)
                split_hi(s + 2)
                if s == 24:
                    act.wait_ge(gelu_in, 1)
                    act.activation(gelu_t, gelu_t, ACT.Tanh, scale=0.7978845608028654).then_inc(gelu_tanh, 1)
                if s == 26:
                    act.wait_ge(la_ready, 1)
                    act.wait_ge(gelu_done, 1)
                    r2 = rr.rearrange("p a b -> p (a b)")
                    link(act.activation(lru_th, r2, ACT.Tanh, scale=-1.0))
                    act.activation(r2, r2, ACT.Exp).then_inc(a_ready, 1)
                if s == 28:
                    act.wait_ge(om_ready, 1)
                    act.activation(lru_th, lru_th, ACT.Sqrt).then_inc(sq_ready, 1)
                if s == 29:
                    act.wait_ge(ot_full, 1)
                    for b in range(3):
                        a = (0, 6, 8)[b]
                        act.activation(mix_hi[:, a:a + 2, :].rearrange("p a (t q) -> p (a t) q", q=P),
                                       backward(ps[:, (2, 3, 6)[b], :].rearrange("p (a q) -> p a q", q=P)), ACT.Copy)\
                            .then_inc(ot_hi, 1)
                if s in (29, 30):
                    a, b = ((0, 8), (8, 2 * (G_LATE - 19)))[s - 29]
                    g = gates[:, a:b, :].rearrange("p a b -> p (a b)")
                    act.activation(g, g, ACT.Sigmoid).then_inc(g_sig, 1)
            evac(N_COL - 1)
            act.wait_ge(hb_ready, 1)
            act.activation(mix_hi[:, 2:6, :], xc, ACT.Copy).then_inc(hb_hi, 1)
            for n in range(T_PA + 2, T_WO):
                split_hi(n)
            split_hi(T_WO)
            split_hi(T_WO + 1)
            for j in range(2):
                act.wait_ge(m_ready, j + 1)
                act.activation(act_hi[:, 4 * j:4 * j + 4, :], merged[:, 4 * j:4 * j + 4, :], ACT.Copy).then_inc(m_hi, 1)
            split_hi(T_WO + 2)
            split_hi(T_WO + 3)
            split_hi(T_FFN)
            split_hi(T_FFN + 1)
            turned_hi(1, act_hi)

            def experts(c0, v0, count, done0, silu_at, t_at):
                def silu(e, c, v):
                    act.wait_ge(tile_used, v * 3 + (c + 1))
                    if not (isinstance(e, int) and e == 0 and isinstance(done0, int) and done0 == 0):
                        act.wait_ge(t_ready, done0 + e)
                    act.activation(silu_at, ps[:, 0, :], ACT.Silu).then_inc(silu_done, 1)

                def hidden(e, c, v):
                    act.wait_ge(t_ready, done0 + e + 1)
                    if c is not None:
                        act.wait_ge(tile_used, v * 3 + (c + 1))
                    act.activation(hid_hi, t_at.rearrange("p (a b) -> p a b", a=2), ACT.Copy).then_inc(hid_h, 1)

                silu(0, c0, v0)
                split_hi(c0 + 2, v0)
                split_hi(c0 + 3, v0)
                hidden(0, None, 0)
                split_hi(c0 + 4, v0)
                split_hi(c0 + 5, v0)
                silu(1, c0 + 2, v0)
                split_hi(c0 + 6, v0)

                def body(e, last):
                    hidden(e - 1, c0 - 2, v0 + e)
                    split_hi(c0 + 1, v0 + e)
                    split_hi(c0 + 2, v0 + e)
                    silu(e, c0 - 1, v0 + e)
                    if not last:
                        split_hi(c0 + 3, v0 + e)

                with act.Fori(2, count - 1) as e:
                    body(e, False)
                body(count - 1, True)
                hidden(count - 1, c0 - 2, v0 + count)

            experts(T_FFN, 0, FFN_E, 0, f_silu, f_t)

            with act.Fori(0, LAYERS) as l:
                v = l * 21
                split_hi(T_L, v)
                split_hi(T_L + 1, v)
                turned_hi(l * 3 + 2, act_hi)
                act.wait_ge(tok_ready, l * 4 + 6)
                act.dma_start(sinks, rows_of(I["attn_sinks_2"][l])).then_inc(lay_in, 16)
                act.dma_start(c_g[:, 0:C_QR], rows_of(I["c_q_norm_g_2"][l])).then_inc(lay_in, 16)
                act.dma_start(c_g[:, C_QR:C_QR + C_KVR], rows_of(I["c_kv_norm_g_2"][l])).then_inc(lay_in, 16)
                act.dma_start(rbias, rows_of(I["router_bias_2"])).then_inc(lay_in, 16)

                def evac_h(j):
                    act.wait_ge(tile_used, l * 63 + (T_L + j + 1))
                    n = min(256, IN2 - L_COLS[j] * 256)
                    c0 = L_COLS[j] * 256
                    act.activation(h[:, :, c0:c0 + n], ps[:, (N_COL + j) % 2, :].rearrange("p (a b) -> p a b", a=2)[:, :, 0:n],
                                   ACT.Copy).then_inc(ring_free, 1)

                def block_out(b, pieces, k=P):
                    act.wait_ge(tb_full, l * 7 + (b + 1))
                    for i, (dst, b0, n) in enumerate(pieces):
                        src = banks(2, 4)[0:k, b0 * P:(b0 + n) * P].rearrange("p (a b) -> p a b", b=S)
                        x = act.activation(dst, src, ACT.Copy)
                    x.then_inc(tb_free, 1)

                one = lambda x: x.rearrange("p (a b) -> p a b", a=1)
                sizes = [KD * min(256, IN2 - t * 256) for t in L_COLS] + [768, 512, TW, TW, TW, TW, 128, TW, TW]
                for j in range(9):
                    if j >= 1:
                        evac_h(j - 1)
                    if j == 6:
                        block_out(0, [(aq_t[:, 0:3, :], 0, 6)])
                    if j == 7:
                        block_out(1, [(aq_t[:, 3:4, :], 0, 2), (ak_t, 2, 4)])
                    if j < 8:
                        split_hi(T_L + j + 2, v, sizes[j + 2])
                block_out(2, [(iq_t, 0, 4), (one(ik_t), 4, 2)])
                act.wait_ge(idx_full, l + 1)
                act.wait_ge(pv_full, l * U_PER + U_L0)
                act.activation(relu_t[0], banks(4, 6), ACT.Relu)
                act.activation(relu_t[1], banks(6, 7), ACT.Relu).then_inc(idx_relu, 1)
                split_hi(T_L + 10, v)
                nu = l * U_PER + U_L0
                for i in range(U_PER + 2):
                    if i == 1:
                        act.wait_ge(tb_full, l * 7 + 4)
                        act.activation(mix_hi[:, 0:3, :], banks(2, 4)[:, 0:768].rearrange("p (a b) -> p a b", b=S), ACT.Copy)\
                            .then_inc(cn_hi, 1)
                    if i == 3:
                        act.wait_ge(tile_used, l * 63 + (T_L + J_UQ + 1))
                        for t in range(TT):
                            act.activation(q_c[:, t, :], ps[:, t, 0:384], ACT.Copy).then_inc(ukv_sb, 1)
                        split_hi(T_L + 11, v)
                    if i == 4:
                        act.wait_ge(tile_used, l * 63 + (T_L + J_UKV + 1))
                        for t in range(TT):
                            act.activation(kv_c[:, t, :], ps[:, t, :], ACT.Copy).then_inc(ukv_sb, 1)
                        split_hi(T_L + 12, v)
                    if i == 5:
                        block_out(4, [(qc_t[0:96, :, :], 0, 8)], 96)
                    if i == 6:
                        block_out(5, [(kc_t[0:96, :, :], 0, 8)], 96)
                    if i == 8:
                        block_out(6, [(bq_t, 0, 4), (one(bk_t), 4, 2)])
                    if i >= 2:
                        probs_out(unit_layer(i - 2), nu + (i - 2))
                    if i < U_PER:
                        exps(unit_layer(i), nu + i)
                turned_hi(l * 3 + 3, mix_hi)
                for j in range(13, 17):
                    split_hi(T_L + j, v, sizes[j])
                turned_hi(l * 3 + 4, act_hi)
                act.wait_ge(tile_used, l * 63 + (T_L + J_RT + 1))
                act.activation(rt[0].rearrange("p a b -> p (a b)"), ps[:, 2, 0:32], ACT.Exp, scale=-1.0).then_inc(rt_exp, 1)
                act.wait_ge(gt_full, l + 1)
                act.activation(gt_sb, ps[0:16, 3, 0:S], ACT.Copy).then_inc(gt_ready, 1)
                experts(T_L + J_MOE, v, N_EXP, l * N_EXP + FFN_E, e_silu, e_t)

        @block.vector
        def _(dve):
            link = Chain(dve, dve_seq)

            def split_lo(c, v=0, n=TW):
                dve.wait_ge(hi_made, v * 3 + (c + 1))
                dve.tensor_tensor(wlo[:, c % 3, 0:n], raw[:, c % 3, 0:n], whi[:, c % 3, 0:n].bitcast(F32), ALU.subtract)\
                    .then_inc(lo_made, 1)

            def turned_lo(n, t, hi, lo):
                for half in range(2):
                    dve.wait_ge(tr_hi, n * 4 + (2 * t + half + 1))
                    a = (slice(None), slice(4 * half, 4 * half + 4), slice(t * P, (t + 1) * P))
                    dve.tensor_tensor(lo[a], ps[:, 2 * t + half, :].rearrange("p (k c) -> p k c", k=4), hi[a].bitcast(F32),
                                      ALU.subtract).then_inc(tr_lo, 1)

            def moments(lk, src, t, eps, square):
                dve.bn_stats(st[:, t, 0:6], src[:, t, 0:512])
                lk(dve.bn_stats(st[:, t, 6:12], src[:, t, 512:1024]), apart)
                lk(dve.bn_aggr(mv[:, t, :], st[:, t, :]))
                if square:
                    lk(dve.scalar_tensor_tensor(out=mv[:, t, 1:2], in0=mv[:, t, 0:1], scalar=mv[:, t, 0:1], in1=mv[:, t, 1:2],
                                                op0=ALU.mult, op1=ALU.add))
                dve.tensor_scalar(var[:, t:t + 1], mv[:, t, 1:2], eps, None, ALU.add).then_inc(var_ready, 1)

            def logits(u, n, lk):
                dve.wait_ge(sc_full, n + 1)
                if not (isinstance(n, int) and n < 2):
                    dve.wait_ge(pt_full, n - 2 if u["one_bank"] else n - 1)
                p, slot = probs_at(u), u["slot"]
                lk(dve.scalar_tensor_tensor(out=p, in0=scores_at(u), scalar=u["scale"], in1=u["bias"], op0=ALU.mult, op1=ALU.add))
                m = 1 if u["joint"] else u["n"]
                ins = dve.tensor_reduce(negm[:, slot, 0:m], p, AX.XY if u["joint"] else AX.X, ALU.max, negate=True)
                if u.get("kind") == "A":
                    x0, x1 = u["heads"]
                    lk(ins)
                    lk(dve.tensor_tensor(negm[:, slot, 0:m], negm[:, slot, 0:m], nsink[:, x0:x1], ALU.min))
                    ins = dve.tensor_tensor(esink[:, slot, 0:m], sinks[:, x0:x1], negm[:, slot, 0:m], ALU.add)
                ins.then_inc(l_ready, 1)

            def outs(u, n, lk):
                dve.wait_ge(pv_full, n + 1)
                slot = u["slot"]
                m = 1 if u["joint"] else u["n"]
                if u.get("kind") == "A":
                    lk(dve.tensor_tensor(den[:, slot, 0:m], den[:, slot, 0:m], esink[:, slot, 0:m], ALU.add))
                lk(dve.reciprocal(rden[:, slot, 0:m], den[:, slot, 0:m]))
                o = u["out"].rearrange("p (n e) -> p n e", e=HD)
                src = pv_at(u).rearrange("p (n e) -> p n e", e=HD)
                dve.tensor_tensor(o, src, spread(rden[:, slot, 0:m], 2, HD), ALU.mult).then_inc(o_ready, 1)

            dve.wait_ge(x_in, 16)
            for t in range(TT):
                moments(link, x_tok, t, EPS_RMS, True)
            dve.wait_ge(gmix_in, 16)
            for t in range(TT):
                dve.wait_ge(rstd_ready, t + 1)
                dve.scalar_tensor_tensor(out=xn1[:, t, :], in0=x_tok[:, t, :], scalar=rstd[:, t:t + 1], in1=g_mix,
                                         op0=ALU.mult, op1=ALU.mult).then_inc(tok_ready, 1)
            split_lo(0)
            split_lo(1)
            dve.wait_ge(prm_full, 1)
            dve.tensor_copy(prm_t[:, :, :], ps[:, 6, 0:8 * LC].rearrange("p (c r) -> p c r", r=8)).then_inc(prm_sb, 1)
            dve.wait_ge(prm_sb, 1)
            link(dve.tensor_scalar(lam[:, 2, :], prm_t[:, :, 7], -1.0, None, ALU.mult))
            dve.tensor_tensor(lam[:, 0, :], lam[:, 2, :], prm_t[:, :, 7], ALU.max).then_inc(lam_abs, 1)
            link(dve.tensor_scalar(lam[:, 2, :], lam[:, 2, :], 0.0, None, ALU.max))
            for t in range(TT):
                turned_lo(0, t, act_hi, act_lo)
            dve.wait_ge(lam_exp, 1)
            link(dve.tensor_scalar(lam[:, 3, :], lam[:, 1, :], 2.0, None, ALU.add))
            link(dve.reciprocal(lam[:, 3, :], lam[:, 3, :]))
            link(dve.tensor_tensor(lam[:, 3, :], lam[:, 3, :], lam[:, 1, :], ALU.mult))
            link(dve.tensor_tensor(lam[:, 4, :], lam[:, 3, :], lam[:, 3, :], ALU.mult))
            link(dve.tensor_scalar(lam[:, 5, :], lam[:, 4, :], 1.0 / 17, None, ALU.mult))
            for k in (15, 13, 11, 9, 7, 5, 3):
                link(dve.scalar_tensor_tensor(out=lam[:, 5, :], in0=lam[:, 5, :], scalar=1.0 / k, in1=lam[:, 4, :],
                                              op0=ALU.add, op1=ALU.mult))
            link(dve.scalar_tensor_tensor(out=lam[:, 5, :], in0=lam[:, 5, :], scalar=1.0, in1=lam[:, 3, :],
                                          op0=ALU.add, op1=ALU.mult))
            link(dve.scalar_tensor_tensor(out=lam[:, 5, :], in0=lam[:, 5, :], scalar=2.0, in1=lam[:, 2, :],
                                          op0=ALU.mult, op1=ALU.add))
            link(dve.tensor_scalar(lam[:, 5, :], lam[:, 5, :], -8.0, None, ALU.mult))

            for s in range(N_COL):
                if s == 9:
                    dve.wait_ge(ext_sb, 1)
                    dve.wait_ge(bias_in, 32)
                if 9 <= s < 17:
                    logits(unit_first(s - 9), s - 9, link)
                if 11 <= s < 19:
                    outs(unit_first(s - 11), s - 11, link)
                if 19 <= s < 25:
                    logits(unit_first(8 + s - 19), 8 + s - 19, link)
                if 21 <= s < 27:
                    outs(unit_first(8 + s - 21), 8 + s - 21, link)
                split_lo(s + 2)
                if s == 17:
                    dve.wait_ge(ring_free, 11)
                    for c in range(LC):
                        link(dve.tensor_scalar(xc[:, c, :], xbp[:, c, 0:S], prm_t[:, c, 0:1], prm_t[:, c, 4:5], ALU.mult, ALU.add))
                        for i in range(1, 4):
                            ins = dve.scalar_tensor_tensor(out=xc[:, c, :], in0=xbp[:, c, i:i + S], scalar=prm_t[:, c, i:i + 1],
                                                           in1=xc[:, c, :], op0=ALU.mult, op1=ALU.add)
                            if c == LC - 1 and i == 3:
                                ins.then_inc(xc_ready, 1)
                            else:
                                link(ins)
                if s == 25:
                    dve.wait_ge(lru_gates, 2)
                    for c in range(LC):
                        ins = dve.tensor_scalar(rr[:, c, :], rr[:, c, :], lam[:, 5, c:c + 1], None, ALU.mult)
                    ins.then_inc(la_ready, 1)
                if s == 27:
                    dve.wait_ge(a_ready, 1)
                    dve.wait_ge(pt_full, 14)
                    r2 = rr.rearrange("p a b -> p (a b)")
                    link(dve.tensor_tensor(lru_q, r2, r2, ALU.mult))
                    dve.scalar_tensor_tensor(out=lru_th, in0=lru_q, scalar=1.0, in1=lru_th, op0=ALU.add, op1=ALU.mult)\
                        .then_inc(om_ready, 1)
                    link(dve.tensor_tensor(ig, ig, xc, ALU.mult))
                if s == 29:
                    dve.wait_ge(sq_ready, 1)
                    th3 = lru_th.rearrange("p (a b) -> p a b", a=LC)
                    link(dve.tensor_tensor(ig, ig, th3, ALU.mult))
                    for c in range(LC):
                        ins = dve.tensor_tensor_scan(xc[:, c, :], rr[:, c, :], ig[:, c, :], 0.0, ALU.mult, ALU.add)
                    link(ins)
                    for b in range(3):
                        a = (0, 6, 8)[b]
                        dve.wait_ge(ot_hi, b + 1)
                        dve.tensor_tensor(mix_lo[:, a:a + 2, :].rearrange("p a (t q) -> p (a t) q", q=P),
                                          backward(ps[:, (2, 3, 6)[b], :].rearrange("p (a q) -> p a q", q=P)),
                                          mix_hi[:, a:a + 2, :].bitcast(F32).rearrange("p a (t q) -> p (a t) q", q=P),
                                          ALU.subtract).then_inc(ot_lo, 1)
            dve.wait_ge(gelu_done, 1)
            dve.tensor_tensor(xc, xc, gb, ALU.mult).then_inc(hb_ready, 1)
            dve.wait_ge(hb_hi, 1)
            dve.tensor_tensor(mix_lo[:, 2:6, :], xc, mix_hi[:, 2:6, :].bitcast(F32), ALU.subtract).then_inc(hb_lo, 1)
            split_lo(T_PA + 2)
            tmp = carve(R3, KD // 2, S)
            dve.wait_ge(tile_used, T_PA + 1)
            dve.wait_ge(g_sig, 2)
            dve.wait_ge(ring_free, N_COL)
            dve.tensor_tensor(merged, banks(0, 4).rearrange("p (a b) -> p a b", b=S), gates[:, 0:8, :], ALU.mult)\
                .then_inc(p_read, 1)
            dve.wait_ge(p_read, 1)
            for i, (c, b0) in enumerate(((T_PB, 4), (T_PB + 1, 6), (T_PC, 0), (T_PC + 1, 2))):
                split_lo(T_PB + 2 + i)
                dve.wait_ge(tile_used, c + 1)
                half = i % 2
                g = gates[:, 8 + 4 * i:12 + 4 * i, :]
                dve.tensor_tensor(tmp, banks(b0, b0 + 2).rearrange("p (a b) -> p a b", b=S), g, ALU.mult).then_inc(p_read, 1)
                dve.wait_ge(p_read, i + 2)
                m = merged[:, 4 * half:4 * half + 4, :]
                ins = dve.tensor_tensor(m, m, tmp, ALU.add)
                if i < 2:
                    link(ins)
                else:
                    ins.then_inc(m_ready, 1)
                    dve.wait_ge(m_hi, half + 1)
                    dve.tensor_tensor(act_lo[:, 4 * half:4 * half + 4, :], m, act_hi[:, 4 * half:4 * half + 4, :].bitcast(F32),
                                      ALU.subtract).then_inc(m_lo, 1)
            for n in range(T_WO + 2, T_FFN + 2):
                split_lo(n)
            def add_and_rms(used, g_at, nth, out, g):
                for t in range(TT):
                    dve.wait_ge(*((early_out, nth) if t == 0 else (tile_used, used)))
                    a = banks(4 + 2 * t, 6 + 2 * t)
                    link(dve.tensor_tensor(x_tok[:, t, :], x_tok[:, t, :], a, ALU.add))
                    moments(link, x_tok, t, EPS_RMS, True)
                    if t == 1:
                        turned_lo(nth, 0, act_hi, act_lo)
                    dve.wait_ge(g_in, g_at)
                    dve.wait_ge(rstd_ready, 2 * nth + 1 + t)
                    dve.scalar_tensor_tensor(out=out[:, t, :], in0=x_tok[:, t, :], scalar=rstd[:, t:t + 1], in1=g,
                                             op0=ALU.mult, op1=ALU.mult).then_inc(tok_ready, 1)
                turned_lo(nth, 1, act_hi, act_lo)

            add_and_rms(T_FFN, 16, 1, xn2, g_ffn)

            def experts(c0, v0, count, done0, silu_at, t_at, gate_of, lk0):
                def product(e, c, v, lk):
                    dve.wait_ge(tile_used, v * 3 + (c + 1))
                    if not (isinstance(e, int) and e == 0 and isinstance(done0, int) and done0 == 0):
                        dve.wait_ge(hid_l, done0 + e)
                    up = ps[:, 1, :].rearrange("p (a b) -> p a b", a=2)
                    t3 = t_at.rearrange("p (a b) -> p a b", a=2)
                    s3 = silu_at.rearrange("p (a b) -> p a b", a=2)
                    if gate_of is not None:
                        lk(dve.tensor_tensor(t3, up, gate_of(e), ALU.mult))
                        dve.wait_ge(silu_done, done0 + e + 1)
                        dve.tensor_tensor(t3, t3, s3, ALU.mult).then_inc(t_ready, 1)
                    else:
                        dve.wait_ge(silu_done, done0 + e + 1)
                        dve.tensor_tensor(t3, up, s3, ALU.mult).then_inc(t_ready, 1)

                def hidden(e):
                    dve.wait_ge(hid_h, done0 + e + 1)
                    dve.tensor_tensor(hid_lo, t_at.rearrange("p (a b) -> p a b", a=2), hid_hi.bitcast(F32),
                                      ALU.subtract).then_inc(hid_l, 1)

                split_lo(c0 + 2, v0)
                if gate_of is not None:
                    dve.wait_ge(gate_in, l_of[0] * 16 + 16)
                product(0, c0 + 1, v0, lk0)
                split_lo(c0 + 3, v0)
                hidden(0)
                split_lo(c0 + 4, v0)
                split_lo(c0 + 5, v0)
                product(1, c0 + 3, v0, lk0)
                split_lo(c0 + 6, v0)

                def body(e, last, lk):
                    hidden(e - 1)
                    split_lo(c0 + 1, v0 + e)
                    split_lo(c0 + 2, v0 + e)
                    product(e, c0, v0 + e, lk)
                    if not last:
                        split_lo(c0 + 3, v0 + e)

                with dve.Fori(2, count - 1) as e:
                    body(e, False, Chain(dve, dve_seq_e, 0, 1, l_of[0] * (N_EXP - 3) + e - 2) if gate_of is not None else None)
                body(count - 1, True, lk0)
                hidden(count - 1)

            l_of = [0]
            experts(T_FFN, 0, FFN_E, 0, f_silu, f_t, None, link)
            split_lo(T_L)
            split_lo(T_L + 1)
            add_and_rms(T_L, 32, 2, x_tok, g_fin)

            def layer(l, last):
                l_of[0] = l
                v = l * 21
                lk = Chain(dve, dve_seq_l, 0, DVE_LINKS, l)
                sizes = [KD * min(256, IN2 - t * 256) for t in L_COLS] + [768, 512, TW, TW, TW, TW, 128, TW, TW]
                for j in range(8):
                    split_lo(T_L + j + 2, v, sizes[j + 2])
                dve.wait_ge(ring_free, l * 8 + (N_COL + 7))
                for t in range(TT):
                    for q, (c0, n) in enumerate(((CQ, C_QR), (CKV, C_KVR))):
                        i = 2 * t + q
                        lk(dve.bn_stats(cst4[:, i, :], h[:, t, c0:c0 + n]), apart)
                        lk(dve.bn_aggr(mv[:, 0, :], cst4[:, i, :]))
                        lk(dve.scalar_tensor_tensor(out=mv[:, 1, 0:1], in0=mv[:, 0, 0:1], scalar=mv[:, 0, 0:1],
                                                    in1=mv[:, 0, 1:2], op0=ALU.mult, op1=ALU.add))
                        ins = dve.tensor_scalar(cvar[:, i:i + 1], mv[:, 1, 0:1], EPS_RMS, None, ALU.add)
                        if i < 3:
                            lk(ins)
                        else:
                            ins.then_inc(cn_var, 1)
                dve.wait_ge(c2_in, 16)
                for t in range(TT):
                    dve.tensor_scalar(wi[:, t, :], h[:, t, IW:IW + 4], IDX_W_SCALE, None, ALU.mult)
                dve.wait_ge(lay_in, l * 64 + 64)
                lk(dve.tensor_scalar(nsink[:, :], sinks[:, :], -1.0, None, ALU.mult))
                dve.wait_ge(cn_rstd, l + 1)
                for t in range(TT):
                    for q, (c0, n, d0) in enumerate(((CQ, C_QR, 0), (CKV, C_KVR, C_QR))):
                        i = 2 * t + q
                        ins = dve.scalar_tensor_tensor(out=cn[:, t, d0:d0 + n], in0=h[:, t, c0:c0 + n],
                                                       scalar=crstd[:, i:i + 1], in1=c_g[:, d0:d0 + n],
                                                       op0=ALU.mult, op1=ALU.mult)
                ins.then_inc(cn_ready, 1)
                split_lo(T_L + 10, v)
                dve.wait_ge(idx_relu, l + 1)
                for x in range(IDX_HEADS):
                    for t, o, w in ((1, 0, S), (0, S, P)):
                        r = relu_t[1 - t][:, x * w:(x + 1) * w]
                        prev = cst[:, C_MC + S - w:C_MC + S] if x == 0 else score[:, o:o + w]
                        lk(dve.scalar_tensor_tensor(out=score[:, o:o + w], in0=r, scalar=wi[:, t, x:x + 1], in1=prev,
                                                    op0=ALU.mult, op1=ALU.add))

                def strike_out(r):
                    for o, w in ((0, S), (S, P)):
                        src = score if r == 0 else pick
                        lk(dve.max(best[:, :], src[:, o:o + w]), apart)
                        lk(dve.match_replace(pick[:, o:o + w], best[:, :], src[:, o:o + w], SEL), apart)

                nu = l * U_PER + U_L0
                for i in range(U_PER + 3):
                    if i == 1:
                        dve.wait_ge(cn_hi, l + 1)
                        dve.tensor_tensor(mix_lo[:, 0:3, :], banks(2, 4)[:, 0:768].rearrange("p (a b) -> p a b", b=S),
                                          mix_hi[:, 0:3, :].bitcast(F32), ALU.subtract).then_inc(cn_lo, 1)
                    if i < U_PER:
                        logits(unit_layer(i), nu + i, lk)
                    if i >= 3:
                        outs(unit_layer(i - 3), nu + (i - 3), lk)
                    if i < 8:
                        strike_out(i)
                    if i == 3:
                        split_lo(T_L + 11, v)
                    if i == 4:
                        split_lo(T_L + 12, v)
                    if i == 7:
                        lk(dve.tensor_scalar(mask_b[:, :], pick[:, :], SEL, 1e30, ALU.is_equal, ALU.mult))
                        for o, w in ((0, S), (S, P)):
                            lk(dve.scalar_tensor_tensor(out=mask_b[:, o:o + w], in0=mask_b[:, o:o + w], scalar=NEG,
                                                        in1=cst[:, C_MC + S - w:C_MC + S], op0=ALU.add, op1=ALU.add))
                for t in range(TT):
                    turned_lo(l * 3 + 3, t, mix_hi, mix_lo)
                for j in range(13, 16):
                    split_lo(T_L + j, v, sizes[j])

                def layer_norm(t, base_r, base_g):
                    dve.wait_ge(rstd_ready, base_r)
                    lk(dve.scalar_tensor_tensor(out=x_tok[:, t, :], in0=x_tok[:, t, :], scalar=mv[:, t, 0:1], in1=ln_g,
                                                op0=ALU.subtract, op1=ALU.mult))
                    dve.scalar_tensor_tensor(out=x_tok[:, t, :], in0=x_tok[:, t, :], scalar=rstd[:, t:t + 1], in1=ln_b,
                                             op0=ALU.mult, op1=ALU.add).then_inc(tok_ready, 1)

                def residual(early, count, base_r, base_g, turned):
                    for t in range(TT):
                        dve.wait_ge(*((early_out, early) if t == 0 else (tile_used, count)))
                        lk(dve.scalar_tensor_tensor(out=x_tok[:, t, :], in0=x_tok[:, t, :], scalar=ALPHA,
                                                    in1=banks(4 + 2 * t, 6 + 2 * t), op0=ALU.mult, op1=ALU.add))
                        moments(lk, x_tok, t, EPS_LN, False)
                        if t == 1 and turned is not None:
                            turned_lo(turned, 0, act_hi, act_lo)
                        dve.wait_ge(gln_in, base_g)
                        layer_norm(t, base_r + t, base_g)
                    if turned is not None:
                        turned_lo(turned, 1, act_hi, act_lo)

                residual(l * 2 + 3, l * 63 + (T_L + J_WO + 4), l * 4 + 7, l * 64 + 32, l * 3 + 4)
                split_lo(T_L + 16, v)
                dve.wait_ge(rt_exp, l + 1)
                sc, bi, ga = rt
                lk(dve.tensor_scalar(sc, sc, 1.0, None, ALU.add))
                lk(dve.reciprocal(sc, sc))
                lk(dve.tensor_tensor(bi, sc, spread(rbias, 1, TT), ALU.add))
                tri = cst[:, C_TRI:C_TRI + 16].rearrange("p (j k) -> p j k", k=4)

                def ranks(val, groups, lk):
                    n = groups * 16
                    gt = pair[:, 0:n].rearrange("p (g j k) -> p g j k", j=4, k=4)
                    eq = pair[:, 64:64 + n].rearrange("p (g j k) -> p g j k", j=4, k=4)
                    v3 = val.rearrange("p (g k) -> p g k", k=4)
                    vk, vj = spread(v3, 2, 4), spread(v3, 3, 4)
                    dve.tensor_tensor(gt, vk, vj, ALU.is_gt)
                    lk(dve.tensor_tensor(eq, vk, vj, ALU.is_equal))
                    lk(dve.tensor_tensor(eq, eq, spread(tri, 1, groups), ALU.mult))
                    lk(dve.tensor_tensor(gt, gt, eq, ALU.add))
                    lk(dve.tensor_reduce(pair[:, 128:128 + groups * 4], pair[:, 0:n].rearrange("p (a k) -> p a k", k=4),
                                         AX.X, ALU.add))
                    return pair[:, 128:128 + groups * 4]

                for t in range(TT):
                    r = ranks(bi[:, t, :], 4, lk)
                    lk(dve.tensor_scalar(ga[:, t, :], r, 1.5, None, ALU.is_lt))
                    lk(dve.tensor_tensor(bi[:, t, :], bi[:, t, :], ga[:, t, :], ALU.mult))
                    lk(dve.tensor_reduce(rg[0][:, t, :], bi[:, t, :].rearrange("p (g k) -> p g k", k=4), AX.X, ALU.add))
                    r = ranks(rg[0][:, t, :], 1, lk)
                    lk(dve.tensor_scalar(rg[1][:, t, :], r, 0.5, None, ALU.is_lt))
                    g3 = ga[:, t, :].rearrange("p (g k) -> p g k", k=4)
                    lk(dve.tensor_tensor(g3, g3, spread(rg[1][:, t, :], 2, 4), ALU.mult))
                    lk(dve.tensor_tensor(ga[:, t, :], ga[:, t, :], sc[:, t, :], ALU.mult))
                    lk(dve.tensor_reduce(rs[:, t:t + 1], ga[:, t, :], AX.X, ALU.add))
                    lk(dve.reciprocal(rs[:, t:t + 1], rs[:, t:t + 1]))
                    ins = dve.tensor_scalar(ga[:, t, :], ga[:, t, :], rs[:, t:t + 1], None, ALU.mult)
                    if t < TT - 1:
                        lk(ins)
                    else:
                        ins.then_inc(gts_ready, 1)
                experts(T_L + J_MOE, v, N_EXP, l * N_EXP + FFN_E, e_silu, e_t,
                        lambda e: spread(gate_bc[:, e, :], 1, 2), lk)
                if not last:
                    split_lo(T_L, v + 21)
                    split_lo(T_L + 1, v + 21)
                residual(l * 2 + 4, l * 63 + (T_L + L_TILES), l * 4 + 9, l * 64 + 64, None if last else l * 3 + 5)
                assert lk.n == DVE_LINKS, lk.n

            with dve.Fori(0, LAYERS - 1) as l:
                layer(l, False)
            layer(LAYERS - 1, True)


_INS = ["x", "rel_bias", "g_mix", "w_in", "conv_w", "conv_b", "lru_wa", "lru_ba", "lru_wx", "lru_bx", "lru_lam", "p_a",
        "p_b", "p_c", "w_out", "g_ffn", "w_gu", "w_down", "g_final", "w_in_2", "attn_sinks_2", "c_q_norm_g_2",
        "c_kv_norm_g_2", "w_uq_2", "w_ukv_2", "w_out_2", "ln1_g_2", "ln1_b_2", "w_router_2", "router_bias_2",
        "w_gate_2", "w_up_2", "w_down_2", "ln2_g_2", "ln2_b_2"]


def kernel(**inputs):
    import concourse.bacc as _bacc
    from concourse.bass_utils import run_bass_kernel_spmd as _run

    nc = _bacc.Bacc("TRN2", target_bir_lowering=False, num_devices=1)
    arrays, aps = {}, {}
    sources = {name: inputs[name] for name in _INS}
    sources.update(shape_constants())
    for name, a in sources.items():
        a = np.ascontiguousarray(a)
        arrays[f"in_{name}"] = a
        aps[name] = nc.dram_tensor(f"in_{name}", a.shape, mybir.dt.from_np(a.dtype), kind="ExternalInput").ap()
    out = nc.dram_tensor("out_0", (1, S, D), F32, kind="ExternalOutput").ap()
    build(nc, aps, out)
    r = _run(nc, [arrays], core_ids=[0])
    return r.results[0]["out_0"]
```
